# Optimizing a Trainium2 kernel written in Bass

```python
import math
import jax, jax.numpy as jnp
from jax import lax
import numpy as np

D_MODEL = 1024
BATCH = 1
SEQ = 1024
DEPTH = 1

N_MIXERS = 3
PLE_DIM = 256
EPS = 1e-6
ATTN_HEADS = 16
ATTN_KV_HEADS = 4
ATTN_HEAD_DIM = 64
WINDOW = 128
ATTN_BLOCK = 128
CONV_WIDTH = 31
SSM_EXPAND = 2
SSM_D_INNER = SSM_EXPAND * D_MODEL
SSM_HEAD_DIM = 64
SSM_HEADS = SSM_D_INNER // SSM_HEAD_DIM
SSM_GROUPS = 8
SSM_STATE = 128
SSM_CONV = 4
SSM_CHUNK = 128
MLP_HIDDEN = 4 * D_MODEL

kernel_name = "hybrid_swa_conformer_ssd_trunk"

def rmsnorm(x, g):
    xf = x.astype(jnp.float32)
    y = xf * lax.rsqrt(jnp.mean(xf * xf, axis=-1, keepdims=True) + EPS)
    return (y * g.astype(jnp.float32)).astype(x.dtype)

def layernorm(x, g, b):
    xf = x.astype(jnp.float32)
    mu = jnp.mean(xf, axis=-1, keepdims=True)
    var = jnp.mean(jnp.square(xf - mu), axis=-1, keepdims=True)
    y = (xf - mu) * lax.rsqrt(var + EPS)
    return (y * g.astype(jnp.float32) + b.astype(jnp.float32)).astype(x.dtype)

def alibi_slopes(n_heads):
    return jnp.exp2(-8.0 * (jnp.arange(n_heads, dtype=jnp.float32) + 1.0) / n_heads)

def causal_dwconv(u, w, b):
    k, c = w.shape
    y = lax.conv_general_dilated(
        u, w[:, None, :].astype(u.dtype), window_strides=(1,), padding=[(k - 1, 0)],
        dimension_numbers=('NWC', 'WIO', 'NWC'), feature_group_count=c)
    return y + b

def sliding_window_attention(u, wqkv, gq, gk, sinks, wo):
    b, s, _ = u.shape
    H, KV, HD, BLK = ATTN_HEADS, ATTN_KV_HEADS, ATTN_HEAD_DIM, ATTN_BLOCK
    G = H // KV
    nb = s // BLK
    qkv = u @ wqkv
    q = qkv[..., :H * HD].reshape(b, s, KV, G, HD)
    k = qkv[..., H * HD:(H + KV) * HD].reshape(b, s, KV, HD)
    v = qkv[..., (H + KV) * HD:].reshape(b, s, KV, HD)
    q = rmsnorm(q, gq)
    k = rmsnorm(k, gk)
    qb = q.reshape(b, nb, BLK, KV, G, HD)

    def band(t):
        tb = t.reshape(b, nb, BLK, KV, HD)
        prev = jnp.pad(tb, ((0, 0), (1, 0), (0, 0), (0, 0), (0, 0)))[:, :-1]
        return jnp.concatenate([prev, tb], axis=2)

    kb, vb = band(k), band(v)
    scores = jnp.einsum('bnqkgd,bnskd->bnkgqs', qb, kb).astype(jnp.float32) * (HD ** -0.5)
    qi = jnp.arange(BLK)
    kj = jnp.arange(2 * BLK)
    dist = qi[:, None] - kj[None, :] + BLK
    kpos = jnp.arange(nb)[:, None] * BLK - BLK + kj[None, :]
    mask = ((dist >= 0) & (dist < WINDOW))[None] & (kpos >= 0)[:, None, :]
    slopes = alibi_slopes(H).reshape(KV, G)
    scores = scores - slopes[:, :, None, None] * dist.astype(jnp.float32)
    scores = jnp.where(mask[None, :, None, None], scores, -jnp.inf)
    sink = sinks.astype(jnp.float32).reshape(KV, G)[:, :, None]
    m = jnp.maximum(scores.max(axis=-1), sink)
    e = jnp.exp(scores - m[..., None])
    probs = e / (e.sum(axis=-1) + jnp.exp(sink - m))[..., None]
    o = jnp.einsum('bnkgqs,bnskd->bnqkgd', probs.astype(v.dtype), vb)
    return o.reshape(b, s, H * HD) @ wo

def conformer_conv_module(u, w_pw1, b_pw1, w_dw, b_dw, ln_g, ln_b, w_pw2, b_pw2):
    a = u @ w_pw1 + b_pw1
    val, gate = jnp.split(a, 2, axis=-1)
    y = val * jax.nn.sigmoid(gate)
    y = causal_dwconv(y, w_dw, b_dw)
    y = layernorm(y, ln_g, ln_b)
    y = jax.nn.silu(y)
    return y @ w_pw2 + b_pw2

def ssd_chunked(xs, dt, A, Bm, Cm):
    b, s, _ = xs.shape
    G, N, P, L = SSM_GROUPS, SSM_STATE, SSM_HEAD_DIM, SSM_CHUNK
    R = SSM_HEADS // G
    nc = s // L
    x = xs.reshape(b, nc, L, G, R, P)
    dtc = dt.reshape(b, nc, L, G, R)
    Bc = Bm.reshape(b, nc, L, G, N)
    Cc = Cm.reshape(b, nc, L, G, N)
    dA = dtc * A.reshape(G, R)
    cs = jnp.cumsum(dA, axis=2)
    x_dt = x * dtc[..., None].astype(x.dtype)
    causal = jnp.arange(L)[:, None] >= jnp.arange(L)[None, :]
    diff = cs[:, :, :, None] - cs[:, :, None, :]
    Lmat = jnp.exp(jnp.where(causal[:, :, None, None], diff, -jnp.inf))
    CB = jnp.einsum('bclgn,bcsgn->bclsg', Cc, Bc)
    y_diag = jnp.einsum('bclsg,bclsgr,bcsgrp->bclgrp', CB, Lmat, x_dt)
    decay_states = jnp.exp(cs[:, :, -1:] - cs)
    states = jnp.einsum('bcsgn,bcsgr,bcsgrp->bcgrpn', Bc, decay_states, x_dt).astype(jnp.float32)
    chunk_decay = jnp.exp(cs[:, :, -1])

    def step(h, inp):
        dec, st = inp
        return dec[..., None, None] * h + st, h

    h0 = jnp.zeros((b, G, R, P, N), jnp.float32)
    _, prev = lax.scan(step, h0, (jnp.moveaxis(chunk_decay, 1, 0), jnp.moveaxis(states, 1, 0)))
    prev = jnp.moveaxis(prev, 0, 1)
    y_off = jnp.einsum('bclgn,bcgrpn,bclgr->bclgrp', Cc, prev, jnp.exp(cs))
    return (y_diag + y_off).reshape(b, s, SSM_HEADS * P).astype(xs.dtype)

def mamba2_mixer(u, w_in, w_conv, b_conv, dt_bias, A_log, Dskip, norm_g, w_out):
    b, s, _ = u.shape
    DI, GN = SSM_D_INNER, SSM_GROUPS * SSM_STATE
    zxbcdt = u @ w_in
    z = zxbcdt[..., :DI]
    xbc = zxbcdt[..., DI:2 * DI + 2 * GN]
    dt_raw = zxbcdt[..., 2 * DI + 2 * GN:]
    xbc = jax.nn.silu(causal_dwconv(xbc, w_conv, b_conv))
    xs = xbc[..., :DI]
    Bm = xbc[..., DI:DI + GN]
    Cm = xbc[..., DI + GN:]
    dt = jax.nn.softplus(dt_raw.astype(jnp.float32) + dt_bias.astype(jnp.float32))
    A = -jnp.exp(A_log.astype(jnp.float32))
    y = ssd_chunked(xs, dt, A, Bm, Cm)
    y = y + (xs.reshape(b, s, SSM_HEADS, SSM_HEAD_DIM) * Dskip[:, None]).reshape(b, s, DI)
    y = rmsnorm(y * jax.nn.silu(z), norm_g)
    return y @ w_out

def sqrelu_mlp(u, w1, w2):
    return jnp.square(jax.nn.relu(u @ w1)) @ w2

def setup_inputs(seed: int = 0) -> dict:
    key = jax.random.key(seed)
    ks = jax.random.split(key, 48)
    ctr = [0]

    def nk():
        ctr[0] += 1
        return ks[ctr[0] - 1]

    def w(shape, fan_in):
        return jax.random.normal(nk(), shape, jnp.float32) * fan_in ** -0.5

    def gain(shape):
        return 1.0 + 0.05 * jax.random.normal(nk(), shape, jnp.float32)

    def bias(shape):
        return 0.02 * jax.random.normal(nk(), shape, jnp.float32)

    n_a = len(range(0, DEPTH, N_MIXERS))
    n_b = len(range(1, DEPTH, N_MIXERS))
    n_c = len(range(2, DEPTH, N_MIXERS))
    D = D_MODEL
    qkv_w = (ATTN_HEADS + 2 * ATTN_KV_HEADS) * ATTN_HEAD_DIM
    in_w = 2 * SSM_D_INNER + 2 * SSM_GROUPS * SSM_STATE + SSM_HEADS
    conv_c = SSM_D_INNER + 2 * SSM_GROUPS * SSM_STATE

    x = jax.random.normal(nk(), (BATCH, SEQ, D), jnp.float32)
    p = jax.random.normal(nk(), (DEPTH, BATCH, SEQ, PLE_DIM), jnp.float32)
    dt0 = jnp.exp(jax.random.uniform(nk(), (n_c, SSM_HEADS), jnp.float32,
                                     minval=math.log(1e-3), maxval=math.log(1e-1)))
    c_dt_bias = dt0 + jnp.log(-jnp.expm1(-dt0))
    c_A_log = jnp.log(jax.random.uniform(nk(), (n_c, SSM_HEADS), jnp.float32, minval=1.0, maxval=16.0))
    return {
        "x": x,
        "p": p,
        "mix_norm_g": gain((DEPTH, D)),
        "mlp_norm_g": gain((DEPTH, D)),
        "ple_norm_g": gain((DEPTH, D)),
        "a_wqkv": w((n_a, D, qkv_w), D),
        "a_q_norm_g": gain((n_a, ATTN_HEAD_DIM)),
        "a_k_norm_g": gain((n_a, ATTN_HEAD_DIM)),
        "a_sinks": 0.5 * jax.random.normal(nk(), (n_a, ATTN_HEADS), jnp.float32),
        "a_wo": w((n_a, ATTN_HEADS * ATTN_HEAD_DIM, D), ATTN_HEADS * ATTN_HEAD_DIM),
        "b_w_pw1": w((n_b, D, 2 * D), D),
        "b_b_pw1": bias((n_b, 2 * D)),
        "b_w_dw": w((n_b, CONV_WIDTH, D), CONV_WIDTH),
        "b_b_dw": bias((n_b, D)),
        "b_ln_g": gain((n_b, D)),
        "b_ln_b": bias((n_b, D)),
        "b_w_pw2": w((n_b, D, D), D),
        "b_b_pw2": bias((n_b, D)),
        "c_w_in": w((n_c, D, in_w), D),
        "c_w_conv": w((n_c, SSM_CONV, conv_c), SSM_CONV),
        "c_b_conv": bias((n_c, conv_c)),
        "c_dt_bias": c_dt_bias,
        "c_A_log": c_A_log,
        "c_D": gain((n_c, SSM_HEADS)),
        "c_norm_g": gain((n_c, SSM_D_INNER)),
        "c_w_out": w((n_c, SSM_D_INNER, D), SSM_D_INNER),
        "m_w1": w((DEPTH, D, MLP_HIDDEN), D),
        "m_w2": w((DEPTH, MLP_HIDDEN, D), MLP_HIDDEN),
        "ple_w_proj": w((DEPTH, PLE_DIM, D), PLE_DIM),
        "ple_w_gate": w((DEPTH, D, D), D),
    }

def reference(x, p, mix_norm_g, mlp_norm_g, ple_norm_g,
              a_wqkv, a_q_norm_g, a_k_norm_g, a_sinks, a_wo,
              b_w_pw1, b_b_pw1, b_w_dw, b_b_dw, b_ln_g, b_ln_b, b_w_pw2, b_b_pw2,
              c_w_in, c_w_conv, c_b_conv, c_dt_bias, c_A_log, c_D, c_norm_g, c_w_out,
              m_w1, m_w2, ple_w_proj, ple_w_gate):
    h = x
    for i in range(DEPTH):
        kind = i % N_MIXERS
        j = i // N_MIXERS
        u = rmsnorm(h, mix_norm_g[i])
        if kind == 0:
            mix = sliding_window_attention(u, a_wqkv[j], a_q_norm_g[j], a_k_norm_g[j],
                                           a_sinks[j], a_wo[j])
        elif kind == 1:
            mix = conformer_conv_module(u, b_w_pw1[j], b_b_pw1[j], b_w_dw[j], b_b_dw[j],
                                        b_ln_g[j], b_ln_b[j], b_w_pw2[j], b_b_pw2[j])
        else:
            mix = mamba2_mixer(u, c_w_in[j], c_w_conv[j], c_b_conv[j], c_dt_bias[j],
                               c_A_log[j], c_D[j], c_norm_g[j], c_w_out[j])
        h = h + mix
        h = h + sqrelu_mlp(rmsnorm(h, mlp_norm_g[i]), m_w1[i], m_w2[i])
        gate = jax.nn.sigmoid(rmsnorm(h, ple_norm_g[i]) @ ple_w_gate[i])
        h = h + gate * (p[i] @ ple_w_proj[i])
    return h


_drawn_inputs = setup_inputs


def setup_inputs(seed=0):
    import zlib

    import numpy as np

    out = dict(_drawn_inputs(seed))
    spreads = {}
    factors = {'ple_norm_g': 24.066, 'a_q_norm_g': 5.186, 'a_k_norm_g': 4.533, 'a_sinks': 51.589}
    for name, (base, spread) in spreads.items():
        noise = np.random.default_rng([zlib.crc32(name.encode()), seed]).standard_normal(out[name].shape)
        drawn = base * np.exp(spread * noise) if base else spread * noise
        out[name] = __import__('jax').numpy.asarray(drawn.astype(out[name].dtype))
    for name, factor in factors.items():
        out[name] = (out[name] * factor).astype(out[name].dtype)
    return out
```

```python
from contextlib import ExitStack

import concourse.bass as bass
from concourse import mybir

F32 = mybir.dt.float32
F32R = mybir.dt.float32r
ALU = mybir.AluOpType
ACT = mybir.ActivationFunctionType
AX = mybir.AxisListType

P = 128
BANK = 512
EPS = 1e-6
HI, LO = 0, 1
PASSES = ((HI, HI), (HI, LO), (LO, HI))
MASKED = -1e30
PARTS = ("kv", "q0", "q8")


def trunk_layer(nc, x, p, mix_g, mlp_g, ple_g, wqkv, gq, gk, sinks, wo, w1, w2, w_proj, w_gate, out):
    T, D = x.shape
    HD = gq.shape[0]
    H = sinks.shape[0]
    QKV = wqkv.shape[1]
    KV = (QKV // HD - H) // 2
    G = H // KV
    NB = T // P
    KT = D // P
    NG = w1.shape[1] // BANK
    MT = BANK // P
    PT = p.shape[1] // P
    NC = D // BANK
    GROUPS = KV
    assert (KT, NB, G, KV, HD, NG, PT, NC) == (8, 8, 4, 4, 64, 8, 2, 2)

    U_QKV, U_WO = 0, 12
    U_W1 = U_WO + KT
    U_MLP = U_W1 + 4
    U_GATE0 = U_W1 + 8 * NG
    U_PROJ = U_GATE0 + 4
    U_GATE1 = U_PROJ + PT
    U_END = U_GATE1 + 4

    def w2_unit(g, k):
        return 8 * g + (U_MLP + k)

    def w1_unit(g, k):
        return 8 * g + (U_W1 + k)

    def rows_of(w, k, col, cols):
        return w[2 * k * P:(2 * k + 2) * P, bass.ds(col, cols)].rearrange("(k p) n -> p k n", p=P)

    with ExitStack() as ctx:
        def sem(name):
            return ctx.enter_context(nc.semaphore(name))

        def sb(name, shape, dt, where=ctx):
            return where.enter_context(nc.sbuf_tensor(name, shape, dt))

        W = sb("W", [P, 3 * 8192], F32R)
        RES = sb("RES", [P, NB, D], F32)
        ring = sb("ring", [P, 2, D], F32)
        gain = sb("gain", [P, D], F32)
        ident = sb("ident", [P, P], F32)
        gq_col = sb("gq_col", [P, 1], F32)
        gq_s = sb("gq_s", [P, 1], F32)
        gk_col = sb("gk_col", [P, 1], F32)
        sink = sb("sink", [P, H], F32)
        nsink = sb("nsink", [P, H], F32)
        half = sb("half", [P, 8], F32)
        warm = sb("warm", [P, 1], F32)
        row_ssq = sb("row_ssq", [P, 1], F32)
        row_var = sb("row_var", [P, 1], F32)
        row_rstd = sb("row_rstd", [P, 1], F32)
        NH = {"kv": KV, "q0": H // 2, "q8": H // 2}
        ssq = {X: sb(f"{X}_ssq", [P, NH[X]], F32) for X in PARTS}
        var = {X: sb(f"{X}_var", [P, NH[X]], F32) for X in PARTS}
        rstd = {X: sb(f"{X}_rstd", [P, NH[X]], F32) for X in PARTS}
        nmax = sb("nmax", [P, 2, G], F32)
        rmax = sb("rmax", [P, 2, G], F32)
        dsink = sb("dsink", [P, 2, G], F32)
        esink = sb("esink", [P, 2, G], F32)
        esum = sb("esum", [P, 2, G], F32)
        denom = sb("denom", [P, 2, G], F32)
        rden = sb("rden", [P, 2, G], F32)

        in_a = ExitStack()
        xb = sb("xb", [P, D], F32, in_a)
        xn = sb("xn", [P, D], F32, in_a)
        xT = sb("xT", [P, 2, KT, P], F32R, in_a)
        qkn = sb("qkn", [P, (H + KV) * HD], F32, in_a)
        sq = sb("sq", [P, BANK], F32, in_a)
        qT = sb("qT", [P, 2, H // 2, P], F32R, in_a)
        kT = sb("kT", [P, 2 * (KV // 2), 2, P], F32R, in_a)
        vnext = sb("vnext", [P, KV * HD], F32, in_a)
        vz = sb("vz", [P, 2, 2, (2 * KV + 1) * HD], F32R, in_a)
        probs = sb("probs", [P, 2, G, 2 * P], F32, in_a)
        pT = sb("pT", [P, 2, 2, BANK], F32R, in_a)
        bias = sb("bias", [P, H, 2 * P], F32, in_a)
        dist = sb("dist", [P, 2 * P], F32, in_a)
        in_a.close()

        in_b = ExitStack()
        uT = sb("uT", [P, 2, KT, T], F32R, in_b)
        hn = sb("hn", [P, D], F32, in_b)
        only_b = ExitStack()
        xr = sb("xr", [P, D], F32, only_b)
        oT = sb("oT", [P, 2, 2, BANK], F32R, only_b)
        only_b.close()
        emb = sb("emb", [P, NB, PT * P], F32, in_b)
        act_buf = sb("act_buf", [P, 2, BANK], F32, in_b)
        in_b.close()
        sig = act_buf

        wq = W[:, 0:2 * KT * QKV].rearrange("p (s k n) -> p s k n", s=2, k=KT)
        wo_s = W[:, 0:2 * KT * D].rearrange("p (s k n) -> p s k n", s=2, k=KT)
        w2_s = W[:, 0:8192].rearrange("p (s k n) -> p s k n", s=2, k=MT)
        hid = W[:, 8192:16384].rearrange("p (s k n) -> p s k n", s=2, k=MT)
        w1_s = W[:, 16384:24576].rearrange("p (s k n) -> p s k n", s=2, k=KT)
        g1_s = W[:, 0:8192].rearrange("p (s k n) -> p s k n", s=2, k=KT)
        wp_s = W[:, 8192:12288].rearrange("p (s k n) -> p s k n", s=2, k=PT)
        eT = W[:, 12288:16384].rearrange("p (s k n) -> p s k n", s=2, k=PT)
        oT_all = RES

        ps = [ctx.enter_context(nc.psum_tensor(f"bank{i}", [P, BANK], F32)) for i in range(8)]
        proj_bank = {"kv": ps[0], "q0": ps[1], "q8": ps[0]}
        score_bank = (ps[2], ps[3])
        pT_bank = (ps[4], ps[5])
        tr_bank, pv_bank = ps[6], ps[7]

        consts_in = sem("consts_in")
        gain_in = sem("gain_in")
        x_in = sem("x_in")
        raw_in = [sem(f"raw_in{i}") for i in range(8)]
        ring_in = [sem(f"ring_in{i}") for i in range(2)]
        emb_in = sem("emb_in")
        out_done = sem("out_done")
        ident_ready = sem("ident_ready")
        ident_zero = sem("ident_zero")
        half_ready = sem("half_ready")
        zeros_ready = sem("zeros_ready")
        dist_step = sem("dist_step")
        bias_first = sem("bias_first")
        bias_full = sem("bias_full")
        scales_ready = sem("scales_ready")
        w_hi = sem("w_hi")
        w_split = sem("w_split")
        x_squared = sem("x_squared")
        x_var = sem("x_var")
        x_rstd = sem("x_rstd")
        xn_ready = sem("xn_ready")
        xT_done = sem("xT_done")
        xT_hi = sem("xT_hi")
        xT_ready = sem("xT_ready")
        projected = {X: sem(f"{X}_projected") for X in PARTS}
        squared = {X: sem(f"{X}_squared") for X in PARTS}
        summed = {X: sem(f"{X}_summed") for X in PARTS}
        var_ready = {X: sem(f"{X}_var_ready") for X in PARTS}
        rstd_ready = {X: sem(f"{X}_rstd_ready") for X in PARTS}
        normed = {X: sem(f"{X}_normed") for X in PARTS}
        turned = {X: sem(f"{X}_turned") for X in PARTS}
        T_hi = {X: sem(f"{X}_T_hi") for X in PARTS}
        T_ready = {X: sem(f"{X}_T_ready") for X in PARTS}
        k_shifted = sem("k_shifted")
        v_staged = sem("v_staged")
        v_shifted = sem("v_shifted")
        v_hi = sem("v_hi")
        v_ready = sem("v_ready")
        scores_ready = sem("scores_ready")
        biased = sem("biased")
        nmax_ready = sem("nmax_ready")
        dsink_ready = sem("dsink_ready")
        exps_done = sem("exps_done")
        denom_ready = sem("denom_ready")
        rden_ready = sem("rden_ready")
        probs_ready = sem("probs_ready")
        probs_turned = sem("probs_turned")
        pT_hi = sem("pT_hi")
        pT_ready = sem("pT_ready")
        pv_done = sem("pv_done")
        attended = sem("attended")
        oT_hi = sem("oT_hi")
        oT_ready = sem("oT_ready")
        wo_half = sem("wo_half")
        xr_in = sem("xr_in")
        h_added = sem("h_added")
        h_squared = sem("h_squared")
        h_var = sem("h_var")
        h_rstd = sem("h_rstd")
        hn_ready = sem("hn_ready")
        uT_done = sem("uT_done")
        uT_hi = sem("uT_hi")
        uT_ready = sem("uT_ready")
        z_ready = sem("z_ready")
        z_relu = sem("z_relu")
        z_squared = sem("z_squared")
        hid_hi = sem("hid_hi")
        hid_ready = sem("hid_ready")
        w2_done = sem("w2_done")
        h_summed = sem("h_summed")
        emb_turned = sem("emb_turned")
        eT_hi = sem("eT_hi")
        eT_ready = sem("eT_ready")
        gate_done = sem("gate_done")
        proj_done = sem("proj_done")
        sig_ready = sem("sig_ready")
        gated = sem("gated")
        out_ready = sem("out_ready")

        passed = sem("passed")

        block = ctx.enter_context(nc.Block())

        def stand(eng, s, value):
            eng.wait_ge(s, value)
            if not isinstance(value, int):
                eng.sem_inc(passed, 1)

        def wait(eng, s, value):
            if not isinstance(value, int) or value > 0:
                eng.wait_ge(s, value)

        def raw_of(u):
            return RES[:, u % 8, :] if u < U_WO else ring[:, u % 2, :]

        def kv_unit(k, s):
            return wq[:, s, 2 * k:2 * k + 2, 2 * BANK:3 * BANK]

        def split_to(kind, k, s):
            return {"kv": lambda: kv_unit(k, s),
                    "q": lambda: wq[:, s, k, 0:D],
                    "wo": lambda: wo_s[:, s, k, :],
                    "w1": lambda: w1_s[:, s, 2 * k:2 * k + 2, :],
                    "w2": lambda: w2_s[:, s, k, :],
                    "gate1": lambda: g1_s[:, s, 2 * k:2 * k + 2, :],
                    "proj": lambda: wp_s[:, s, k, :]}[kind]()

        def shaped(raw, like):
            return raw if len(like.shape) == 2 else raw.rearrange("p (k n) -> p k n", k=like.shape[1])

        def q_rows(j):
            return slice((j % 2) * HD, (j % 2 + 1) * HD)

        def pos(r):
            return (r % 2) * 2 + r // 2

        def b_banks(odd):
            return (ps[6], ps[7]) if odd else (ps[4], ps[5])

        def d_banks(odd):
            return (ps[2], ps[3]) if odd else (ps[0], ps[1])

        @block.sync
        def _(sp):
            sp.dma_start(xb[:], x[0:P, :]).then_inc(x_in, 16)
            sp.dma_start(gain[:], mix_g.partition_broadcast(P)).then_inc(gain_in, 16)
            for u in range(U_WO):
                if u >= 8:
                    sp.wait_ge(w_split, u - 8 + 1)
                dst = RES[:, u % 8, :]
                if u < 4:
                    sp.dma_start(dst.rearrange("p (k n) -> p k n", k=2),
                                 rows_of(wqkv, u, H * HD, 2 * KV * HD)).then_inc(raw_in[u % 8], 16)
                else:
                    sp.dma_start(dst, wqkv[(u - 4) * P:(u - 3) * P, 0:H * HD]).then_inc(raw_in[u % 8], 16)
            for place in (0, 1):
                wu = U_WO + place
                sp.dma_start(ring[:, place, :], wo[place * P:(place + 1) * P, :]).then_inc(ring_in[place], 16)
            with sp.Fori(1, NB) as b:
                sp.wait_ge(xn_ready, b)
                sp.dma_start(xb[:], x[bass.ds(b * P, P), :]).then_inc(x_in, 16)
            sp.wait_ge(xn_ready, NB)
            sp.dma_start(gain[:], mlp_g.partition_broadcast(P)).then_inc(gain_in, 16)
            for k in range(2, KT):
                sp.wait_ge(w_split, U_WO + k - 1)
                sp.dma_start(ring[:, k % 2, :], wo[k * P:(k + 1) * P, :]).then_inc(ring_in[k % 2], 16)
            sp.wait_ge(attended, NB * GROUPS)
            sp.dma_start(xr[:], x[0:P, :]).then_inc(xr_in, 16)
            for k in range(4):
                sp.wait_ge(w_split, U_W1 + k - 1)
                sp.dma_start(ring[:, k % 2, :].rearrange("p (k n) -> p k n", k=2),
                             rows_of(w1, k, 0, BANK)).then_inc(ring_in[k % 2], 16)
            with sp.Fori(1, NB) as b:
                sp.wait_ge(h_added, 2 * b)
                sp.dma_start(xr[:], x[bass.ds(b * P, P), :]).then_inc(xr_in, 16)
            sp.wait_ge(wo_half, 2 * NB)
            sp.wait_ge(h_added, 2 * NB)
            sp.dma_start(emb[:], p.rearrange("(b p) n -> p b n", p=P)).then_inc(emb_in, 16)
            sp.wait_ge(hn_ready, NB)
            sp.dma_start(gain[:], ple_g.partition_broadcast(P)).then_inc(gain_in, 16)

            def load_group(g, last):
                for k in range(MT):
                    sp.wait_ge(w_split, w2_unit(g, k) - 1)
                    sp.dma_start(ring[:, k % 2, :], w2[bass.ds(g * BANK + k * P, P), :]).then_inc(ring_in[k % 2], 16)
                for k in range(4):
                    sp.wait_ge(w_split, w1_unit(g, k) + 7)
                    src = rows_of(w_gate, k, 0, BANK) if last else rows_of(w1, k, g * BANK + BANK, BANK)
                    sp.dma_start(ring[:, k % 2, :].rearrange("p (k n) -> p k n", k=2), src).then_inc(ring_in[k % 2], 16)

            with sp.Fori(0, NG - 1) as g:
                load_group(g, False)
            load_group(NG - 1, True)
            for k in range(PT):
                sp.wait_ge(w_split, U_PROJ + k - 1)
                sp.dma_start(ring[:, k % 2, :], w_proj[k * P:(k + 1) * P, :]).then_inc(ring_in[k % 2], 16)
            for k in range(4):
                sp.wait_ge(w_split, U_GATE1 + k - 1)
                sp.dma_start(ring[:, k % 2, :].rearrange("p (k n) -> p k n", k=2),
                             rows_of(w_gate, k, BANK, BANK)).then_inc(ring_in[k % 2], 16)
            for s in range(NB * NC):
                c, b = s // NB, s % NB
                sp.wait_ge(out_ready, s + 1)
                sp.dma_start(out[b * P:(b + 1) * P, c * BANK:(c + 1) * BANK],
                             RES[:, b, c * BANK:(c + 1) * BANK]).then_inc(out_done, 16)
            sp.wait_ge(out_done, 16 * NB * NC)

        @block.gpsimd
        def _(pool):
            pool.memset(half[:], -0.5).then_inc(half_ready, 1)
            pool.memset(ident[:], 0.0).then_inc(ident_zero, 1)
            pool.wait_ge(ident_zero, 1)
            pool.affine_select(out=ident[:], in_=ident[:], compare_op=ALU.not_equal, fill=1.0,
                               base=0, pattern=[[-1, P]], channel_multiplier=1).then_inc(ident_ready, 1)
            pool.wait_ge(half_ready, 1)

            def row_norm(squares, var_sem, rstd_sem, b):
                stand(pool, squares, b + 1)
                pool.tensor_scalar(row_var[:], row_ssq[:], 1.0 / D, EPS, ALU.mult, ALU.add).then_inc(var_sem, 1)
                pool.wait_ge(var_sem, b + 1)
                pool.tensor_tensor(row_rstd[:], row_var[:], half[:, 0:1], ALU.pow).then_inc(rstd_sem, 1)

            def head_norm(X, b):
                stand(pool, summed[X], b + 1)
                pool.tensor_scalar(var[X][:], ssq[X][:], 1.0 / HD, EPS, ALU.mult, ALU.add).then_inc(var_ready[X], 1)
                pool.wait_ge(var_ready[X], b + 1)
                pool.tensor_tensor(rstd[X][:], var[X][:], half[:, 0:NH[X]], ALU.pow).then_inc(rstd_ready[X], 1)

            row_norm(x_squared, x_var, x_rstd, 0)
            pool.memset(vz[:].bitcast(F32), 0.0).then_inc(zeros_ready, 1)
            pool.memset(kT[:].bitcast(F32), 0.0).then_inc(zeros_ready, 1)
            pool.iota(dist[:], pattern=[[-1, 2 * P]], base=P, channel_multiplier=1,
                      allow_small_or_imprecise_dtypes=True).then_inc(dist_step, 1)
            pool.wait_ge(dist_step, 1)
            pool.affine_select(out=dist[:], in_=dist[:], compare_op=ALU.is_ge, fill=-1e3 * MASKED,
                               base=P, pattern=[[-1, 2 * P]], channel_multiplier=1).then_inc(dist_step, 1)
            pool.wait_ge(dist_step, 2)
            pool.affine_select(out=dist[:], in_=dist[:], compare_op=ALU.is_ge, fill=-1e3 * MASKED,
                               base=-1, pattern=[[1, 2 * P]], channel_multiplier=-1).then_inc(dist_step, 1)
            pool.wait_ge(dist_step, 3)

            def bias_of(h, cols, ready):
                slope = 2.0 ** (-8.0 * (h + 1) / H)
                pool.tensor_scalar(bias[:, h, cols], dist[:, cols], -slope, 1.0, ALU.mult, ALU.mult).then_inc(ready, 1)

            pool.memset(bias[:, :, 0:P], MASKED).then_inc(bias_first, 1)
            for h in range(H):
                bias_of(h, slice(P, 2 * P), bias_first)
            for X in PARTS:
                head_norm(X, 0)

            def body(n):
                row_norm(x_squared, x_var, x_rstd, n + 1)
                for X in PARTS:
                    head_norm(X, n + 1)

            row_norm(x_squared, x_var, x_rstd, 1)
            for j in range(GROUPS):
                pool.wait_ge(biased, G * (j + 1))
                for r in range(G):
                    bias_of(G * j + r, slice(0, P), bias_full)
                if j >= 1:
                    head_norm(PARTS[j - 1], 1)
            with pool.Fori(1, NB - 1) as n:
                body(n)
            with pool.Fori(0, 2 * NB) as b:
                row_norm(h_squared, h_var, h_rstd, b)

        @block.scalar
        def _(act):
            def hi_unit(u, kind, k, free=()):
                for s, v in free:
                    wait(act, s, v)
                if isinstance(u, int) and u < U_WO:
                    act.wait_ge(raw_in[u % 8], 16 * (u // 8 + 1))
                    raw = RES[:, u % 8, :]
                else:
                    act.wait_ge(ring_in[k % 2], (u - (U_WO + k % 2)) * 8 + 16)
                    raw = ring[:, k % 2, :]
                dst = split_to(kind, k, HI)
                nc.scalar.activation(dst, shaped(raw, dst), ACT.Copy).then_inc(w_hi, 1)

            def x_squares(b):
                act.wait_ge(x_in, 16 * (b + 1))
                wait(act, xT_done, 2 * b)
                nc.scalar.activation(xn[:], xb[:], ACT.Square, accum_out=row_ssq[:]).then_inc(x_squared, 1)

            def xT_hi_half(b, hf):
                act.wait_ge(xT_done, 2 * b + (1 + hf))
                wait(act, projected["q8"], b)
                bank = ps[6] if hf == 0 else ps[1]
                nc.scalar.activation(xT[:, HI, 4 * hf:4 * hf + 4, :], bank[:].rearrange("p (k n) -> p k n", k=4),
                                     ACT.Copy).then_inc(xT_hi, 1)

            def part_squares(X, b):
                act.wait_ge(projected[X], b + 1)
                if X == "kv":
                    wait(act, summed["q8"], b)
                else:
                    act.wait_ge(summed["kv" if X == "q0" else "q0"], b + 1)
                cols = NH[X] * HD
                nc.scalar.activation(sq[:, 0:cols], proj_bank[X][:, 0:cols], ACT.Square).then_inc(squared[X], 1)

            def stage_v(b):
                act.wait_ge(projected["kv"], b + 1)
                wait(act, v_ready, b)
                nc.scalar.activation(vnext[:], ps[0][:, KV * HD:2 * KV * HD], ACT.Copy).then_inc(v_staged, 1)

            def values(slot, s):
                return vz[:, slot, s, HD:(2 * KV + 1) * HD].rearrange("p (v a d) -> p v a d", v=KV, a=2)[:, :, 0, :]

            def v_hi_part(b):
                act.wait_ge(v_staged, b + 1)
                if isinstance(b, int) and b == 0:
                    act.wait_ge(zeros_ready, 2)
                wait(act, v_shifted, b)
                nc.scalar.activation(values(1, HI), vnext[:].rearrange("p (v d) -> p v d", v=KV),
                                     ACT.Copy).then_inc(v_hi, 1)

            def T_hi_part(X, b):
                act.wait_ge(turned[X], b + 1)
                if X == "kv":
                    if isinstance(b, int) and b == 0:
                        act.wait_ge(zeros_ready, 2)
                    wait(act, k_shifted, b)
                    nc.scalar.activation(kT[:, 0:2, 1, :], tr_bank[:, 0:2 * P].rearrange("p (a n) -> p a n", a=2),
                                         ACT.Copy, scale=gk_col[:]).then_inc(T_hi[X], 1)
                else:
                    wait(act, scores_ready, 8 * b - (4 if X == "q0" else 0))
                    a = 0 if X == "q0" else 4
                    nc.scalar.activation(qT[:, HI, a:a + 4, :], tr_bank[:].rearrange("p (a n) -> p a n", a=4),
                                         ACT.Copy, scale=gq_s[:]).then_inc(T_hi[X], 1)

            def exps(n, j):
                t, i = 4 * n + j, j % 2
                act.wait_ge(nmax_ready, t + 1)
                for r in range(G):
                    nc.scalar.activation(probs[:, i, r, :], probs[:, i, r, :], ACT.Exp, bias=nmax[:, i, r:r + 1],
                                         accum_out=esum[:, i, r:r + 1])
                act.wait_ge(dsink_ready, t + 1)
                nc.scalar.activation(esink[:, i, :], dsink[:, i, :], ACT.Exp).then_inc(exps_done, 1)

            def pT_hi_part(t):
                for kt in range(2):
                    act.wait_ge(probs_turned, 2 * t + (1 + kt))
                    wait(act, pv_done, t)
                    nc.scalar.activation(pT[:, HI, kt, :], pT_bank[kt][:], ACT.Copy).then_inc(pT_hi, 1)

            def attention_out(n, j):
                t = 4 * n + j
                act.wait_ge(w_split, U_WO)
                act.wait_ge(pv_done, t + 1)
                dst = RES[:].rearrange("p b n -> p (b n)")[:, bass.ds(n * D + j * 2 * P, 2 * P)]
                nc.scalar.activation(dst, pv_bank[:, 0:2 * P], ACT.Copy).then_inc(attended, 1)

            def before(n, j, lag):
                return (n, j - lag) if j >= lag else (n - 1, j - lag + GROUPS)

            def body(n, first=False, last=False):
                for j in range(GROUPS):
                    t = 4 * n + j
                    if j == 0:
                        if not last:
                            x_squares(n + 1)
                        if not first:
                            attention_out(*before(n, j, 2))
                            pT_hi_part(t - 1)
                        if not last:
                            xT_hi_half(n + 1, 0)
                            xT_hi_half(n + 1, 1)
                        exps(n, j)
                        T_hi_part("q8", n)
                        continue
                    exps(n, j)
                    if j == 1:
                        if not last:
                            part_squares("kv", n + 1)
                        if not first:
                            attention_out(*before(n, j, 2))
                        v_hi_part(n)
                        pT_hi_part(t - 1)
                        if not last:
                            stage_v(n + 1)
                    if j == 2:
                        if not last:
                            part_squares("q0", n + 1)
                        attention_out(*before(n, j, 2))
                        pT_hi_part(t - 1)
                    if j == 3:
                        if not last:
                            T_hi_part("kv", n + 1)
                            part_squares("q8", n + 1)
                        attention_out(*before(n, j, 2))
                        pT_hi_part(t - 1)
                        if not last:
                            T_hi_part("q0", n + 1)
                    if last:
                        for k in range(3 * (j - 1), min(3 * j, KT)):
                            hi_unit(U_WO + k, "wo", k, [(projected["q8"], NB)])

            for col, g in ((gq_col, gq), (gk_col, gk)):
                for a in range(2):
                    act.dma_start(col[a * HD:(a + 1) * HD, :], g.rearrange("(d a) -> d a", a=1)).then_inc(consts_in, 16)
            act.dma_start(sink[:], sinks.partition_broadcast(P)).then_inc(consts_in, 16)
            act.wait_ge(half_ready, 1)
            nc.scalar.activation(warm[:], half[:, 0:1], ACT.Exp)
            x_squares(0)
            for u in range(4):
                hi_unit(u, "kv", u)
            xT_hi_half(0, 0)
            xT_hi_half(0, 1)
            for u in range(4, U_WO):
                hi_unit(u, "q", u - 4)
            part_squares("kv", 0)
            stage_v(0)
            act.wait_ge(scales_ready, 1)
            part_squares("q0", 0)
            T_hi_part("kv", 0)
            part_squares("q8", 0)
            T_hi_part("q0", 0)
            body(0, first=True)
            with act.Fori(1, NB - 1) as n:
                body(n)
            body(NB - 1, last=True)
            last_t = NB * GROUPS - 1
            attention_out(NB - 1, GROUPS - 2)
            pT_hi_part(last_t)
            attention_out(NB - 1, GROUPS - 1)

            def oT_hi_half(b, hf):
                act.wait_ge(attended, NB * GROUPS)
                wait(act, wo_half, 2 * b + (hf - 1))
                src = RES[:].rearrange("p b n -> p (b n)")[:, bass.ds(b * D + hf * BANK, BANK)]
                nc.scalar.activation(oT[:, hf, HI, :], src, ACT.Copy).then_inc(oT_hi, 1)

            def h_squares(b, summed_sem, base, bb):
                act.wait_ge(attended, NB * GROUPS)
                wait(act, uT_done, 2 * bb)
                stand(act, summed_sem, base + 2 * b + 2)
                src = RES[:].rearrange("p b n -> p (b n)")[:, bass.ds(b * D, D)]
                nc.scalar.activation(hn[:], src, ACT.Square, accum_out=row_ssq[:]).then_inc(h_squared, 1)

            def uT_hi_part(b, bb, banks):
                for hf in range(2):
                    act.wait_ge(pv_done, NB * GROUPS)
                    act.wait_ge(uT_done, 2 * bb + (hf + 1))
                    nc.scalar.activation(uT[:, HI, 4 * hf:4 * hf + 4, bass.ds(b * P, P)],
                                         banks[hf][:].rearrange("p (k n) -> p k n", k=4),
                                         ACT.Copy).then_inc(uT_hi, 1)

            def block_b(b, odd, first=False, last=False):
                if not last:
                    oT_hi_half(b + 1, 0)
                if not first:
                    uT_hi_part(b - 1, b - 1, b_banks(not odd))
                if not last:
                    oT_hi_half(b + 1, 1)
                h_squares(b, h_added, 0, b)

            oT_hi_half(0, 0)
            oT_hi_half(0, 1)
            block_b(0, False, first=True)
            for k in range(2):
                hi_unit(w1_unit(0, k), "w1", k)
            with act.Fori(0, (NB - 2) // 2) as i:
                block_b(2 * i + 1, True)
                block_b(2 * i + 2, False)
            for k in range(2, 4):
                hi_unit(w1_unit(0, k), "w1", k)
            block_b(NB - 1, True, last=True)

            def relu(g, i):
                act.wait_ge(z_ready, 8 * g + (i + 1))
                wait(act, hid_ready, 8 * g + (i - 1))
                nc.scalar.activation(act_buf[:, i % 2, :], ps[i % 4][:], ACT.Relu).then_inc(z_relu, 1)

            def hid_hi_part(g, i):
                act.wait_ge(z_squared, 8 * g + (i + 1))
                wait(act, w2_done, 16 * g)
                nc.scalar.activation(hid[:, HI, i % MT, (i // MT) * BANK:(i // MT + 1) * BANK],
                                     act_buf[:, i % 2, :], ACT.Copy).then_inc(hid_hi, 1)

            def group(g, first=False, last=False):
                for i in range(2 * MT):
                    if first and i == 0:
                        act.wait_ge(wo_half, 2 * NB)
                    relu(g, i)
                    hid_hi_part(g, i)
                    if first and i == 0:
                        uT_hi_part(NB - 1, NB - 1, b_banks(True))
                    if i % 2 == 0:
                        hi_unit(w2_unit(g, i // 2), "w2", i // 2, [(w2_done, 16 * g)])
                for a in range(NB):
                    if a % 2 == 0:
                        hi_unit(w1_unit(g, a // 2) + 8, "w1", a // 2, [(z_ready, 8 * g + 8)])
                    if last:
                        if a >= 1:
                            uT_hi_part_d(a - 1)
                        h_squares(a, h_summed, 16 * g, NB + a)

            def uT_hi_part_d(b):
                uT_hi_part(b, NB + b, d_banks(b % 2))

            group(0, first=True)
            with act.Fori(1, NG - 1) as g:
                group(g)
            group(NG - 1, last=True)

            def gate(s):
                act.wait_ge(gate_done, s + 1)
                wait(act, out_ready, s - 1)
                if s < 2:
                    act.wait_ge(hid_ready, 8 * NG)
                nc.scalar.activation(sig[:, s % 2, :], ps[4 + s % 2][:], ACT.Sigmoid).then_inc(sig_ready, 1)

            gate(0)
            uT_hi_part_d(NB - 1)
            gate(1)
            for q in range(4):
                act.wait_ge(emb_turned, q + 1)
                act.wait_ge(w2_done, 16 * NG)
                nc.scalar.activation(eT[:, HI, q // 2, (q % 2) * BANK:(q % 2 + 1) * BANK], ps[q][:],
                                     ACT.Copy).then_inc(eT_hi, 1)
            for k in range(PT):
                hi_unit(U_PROJ + k, "proj", k, [(w2_done, 16 * NG)])
            for s in range(2, NB * NC):
                gate(s)
                if s < 6:
                    hi_unit(U_GATE1 + s - 2, "gate1", s - 2, [(w2_done, 16 * NG)])

        @block.vector
        def _(dve):
            def lo_unit(u, kind, k):
                raw = RES[:, u % 8, :] if isinstance(u, int) and u < U_WO else ring[:, k % 2, :]
                dst, top = split_to(kind, k, LO), split_to(kind, k, HI)
                dve.wait_ge(w_hi, u + 1)
                nc.vector.tensor_tensor(dst, shaped(raw, dst), top.bitcast(F32), ALU.subtract).then_inc(w_split, 1)

            def x_norm(b):
                dve.wait_ge(x_rstd, b + 1)
                nc.vector.scalar_tensor_tensor(out=xn[:], in0=xb[:], scalar=row_rstd[:], in1=gain[:],
                                               op0=ALU.mult, op1=ALU.mult).then_inc(xn_ready, 1)

            def xT_lo_half(b, hf):
                dve.wait_ge(xT_hi, 2 * b + (1 + hf))
                bank = ps[6] if hf == 0 else ps[1]
                nc.vector.tensor_tensor(xT[:, LO, 4 * hf:4 * hf + 4, :], bank[:].rearrange("p (k n) -> p k n", k=4),
                                        xT[:, HI, 4 * hf:4 * hf + 4, :].bitcast(F32),
                                        ALU.subtract).then_inc(xT_ready, 1)

            def head_sums(X, b):
                dve.wait_ge(squared[X], b + 1)
                cols = NH[X] * HD
                nc.vector.tensor_reduce(ssq[X][:], sq[:, 0:cols].rearrange("p (h d) -> p h d", d=HD), AX.X,
                                        ALU.add).then_inc(summed[X], 1)

            def head_scale(X, b):
                dve.wait_ge(rstd_ready[X], b + 1)
                wait(dve, turned[X], b)
                if X == "kv":
                    dve.wait_ge(v_staged, b + 1)
                    o = qkn[:, H * HD:(H + KV) * HD].rearrange("p (h d) -> p h d", d=HD)
                    i = ps[0][:, 0:KV * HD].rearrange("p (h d) -> p h d", d=HD)
                    s = rstd[X][:].unsqueeze(2).to_broadcast([P, KV, HD])
                else:
                    a = 0 if X == "q0" else BANK
                    o = qkn[:, a:a + BANK].rearrange("p (r a d) -> p r a d", r=G, a=2)
                    i = proj_bank[X][:].rearrange("p (a r d) -> p r a d", a=2, r=G)
                    s = rstd[X][:].rearrange("p (a r) -> p r a", a=2).unsqueeze(3).to_broadcast([P, G, 2, HD])
                nc.vector.tensor_tensor(o, i, s, ALU.mult).then_inc(normed[X], 1)

            def T_lo_part(X, b):
                dve.wait_ge(T_hi[X], b + 1)
                if X == "kv":
                    nc.vector.scalar_tensor_tensor(
                        out=kT[:, 2:4, 1, :], in0=tr_bank[:, 0:2 * P].rearrange("p (a n) -> p a n", a=2),
                        scalar=gk_col[:], in1=kT[:, 0:2, 1, :].bitcast(F32), op0=ALU.mult,
                        op1=ALU.subtract).then_inc(T_ready[X], 1)
                else:
                    a = 0 if X == "q0" else 4
                    nc.vector.scalar_tensor_tensor(
                        out=qT[:, LO, a:a + 4, :], in0=tr_bank[:].rearrange("p (a n) -> p a n", a=4),
                        scalar=gq_s[:], in1=qT[:, HI, a:a + 4, :].bitcast(F32), op0=ALU.mult,
                        op1=ALU.subtract).then_inc(T_ready[X], 1)

            def shift_k(b):
                dve.wait_ge(scores_ready, 8 * b)
                nc.vector.tensor_copy(kT[:, :, 0, :], kT[:, :, 1, :].bitcast(F32)).then_inc(k_shifted, 1)

            def shift_v(b):
                dve.wait_ge(pv_done, 4 * b)
                nc.vector.tensor_copy(vz[:, 0], vz[:, 1].bitcast(F32)).then_inc(v_shifted, 1)

            def v_lo_part(b):
                def values(s):
                    return vz[:, 1, s, HD:(2 * KV + 1) * HD].rearrange("p (v a d) -> p v a d", v=KV, a=2)[:, :, 0, :]
                dve.wait_ge(v_hi, b + 1)
                nc.vector.tensor_tensor(values(LO), vnext[:].rearrange("p (v d) -> p v d", v=KV),
                                        values(HI).bitcast(F32), ALU.subtract).then_inc(v_ready, 1)

            def add_bias(n, j, first):
                t, i = 4 * n + j, j % 2
                for r in range(G):
                    if r == 0:
                        if first:
                            dve.wait_ge(bias_first, 1 + H)
                        else:
                            dve.wait_ge(bias_full, G * (j + 1))
                        wait(dve, probs_turned, 2 * t - 2)
                    if r % 2 == 0:
                        stand(dve, scores_ready, 2 * t + (1 + r // 2))
                    nc.vector.tensor_tensor_reduce(
                        probs[:, i, r, :], score_bank[r // 2][:, (r % 2) * 2 * P:(r % 2 + 1) * 2 * P],
                        bias[:, G * j + r, :], 1.0, 0.0, ALU.add, ALU.max, rmax[:, i, r:r + 1]).then_inc(biased, 1)
                dve.wait_ge(biased, 4 * t + 4)
                nc.vector.scalar_tensor_tensor(out=nmax[:, i, :], in0=rmax[:, i, :], scalar=-1.0,
                                               in1=nsink[:, G * j:G * j + G], op0=ALU.mult,
                                               op1=ALU.min).then_inc(nmax_ready, 1)
                dve.wait_ge(nmax_ready, t + 1)
                nc.vector.tensor_tensor(dsink[:, i, :], nmax[:, i, :], nsink[:, G * j:G * j + G],
                                        ALU.subtract).then_inc(dsink_ready, 1)

            def scale_probs(n, j):
                t, i = 4 * n + j, j % 2
                dve.wait_ge(exps_done, t + 1)
                nc.vector.tensor_tensor(denom[:, i, :], esum[:, i, :], esink[:, i, :], ALU.add).then_inc(denom_ready, 1)
                dve.wait_ge(denom_ready, t + 1)
                nc.vector.reciprocal(rden[:, i, :], denom[:, i, :]).then_inc(rden_ready, 1)
                dve.wait_ge(rden_ready, t + 1)
                nc.vector.tensor_tensor(probs[:, i], probs[:, i], rden[:, i, :].unsqueeze(2).to_broadcast([P, G, 2 * P]),
                                        ALU.mult).then_inc(probs_ready, 1)

            def pT_lo_part(t):
                for kt in range(2):
                    dve.wait_ge(pT_hi, 2 * t + (1 + kt))
                    nc.vector.tensor_tensor(pT[:, LO, kt, :], pT_bank[kt][:], pT[:, HI, kt, :].bitcast(F32),
                                            ALU.subtract).then_inc(pT_ready, 1)

            def body(n, first=False, last=False):
                for j in range(GROUPS):
                    t = 4 * n + j
                    if j == 0:
                        if not last:
                            x_norm(n + 1)
                        add_bias(n, j, first)
                        if not first:
                            pT_lo_part(t - 1)
                        head_scale("q8", n)
                        if not last:
                            xT_lo_half(n + 1, 0)
                            xT_lo_half(n + 1, 1)
                        scale_probs(n, j)
                        T_lo_part("q8", n)
                    if j == 1:
                        add_bias(n, j, first)
                        scale_probs(n, j)
                        if not last:
                            head_sums("kv", n + 1)
                        if not first:
                            shift_v(n)
                        v_lo_part(n)
                        pT_lo_part(t - 1)
                    if j == 2:
                        if not last:
                            head_scale("kv", n + 1)
                        add_bias(n, j, first)
                        scale_probs(n, j)
                        if not last:
                            head_sums("q0", n + 1)
                        pT_lo_part(t - 1)
                    if j == 3:
                        if not last:
                            head_scale("q0", n + 1)
                        add_bias(n, j, first)
                        if not last:
                            shift_k(n + 1)
                        scale_probs(n, j)
                        if not last:
                            T_lo_part("kv", n + 1)
                            head_sums("q8", n + 1)
                        pT_lo_part(t - 1)
                        if not last:
                            T_lo_part("q0", n + 1)
                    if last and j >= 1:
                        for k in range(3 * (j - 1), min(3 * j, KT)):
                            lo_unit(U_WO + k, "wo", k)

            dve.wait_ge(consts_in, 16 * 5)
            nc.vector.tensor_scalar(nsink[:], sink[:], -1.0, None, ALU.mult)
            nc.vector.tensor_scalar(gq_s[:], gq_col[:], HD ** -0.5, None, ALU.mult).then_inc(scales_ready, 1)
            dve.wait_ge(gain_in, 16)
            x_norm(0)
            for u in range(4):
                lo_unit(u, "kv", u)
            xT_lo_half(0, 0)
            xT_lo_half(0, 1)
            for u in range(4, U_WO):
                lo_unit(u, "q", u - 4)
            head_sums("kv", 0)
            head_scale("kv", 0)
            head_sums("q0", 0)
            head_scale("q0", 0)
            T_lo_part("kv", 0)
            head_sums("q8", 0)
            T_lo_part("q0", 0)
            body(0, first=True)
            with dve.Fori(1, NB - 1) as n:
                body(n)
            body(NB - 1, last=True)
            pT_lo_part(NB * GROUPS - 1)

            flat = RES[:].rearrange("p b n -> p (b n)")

            def oT_lo_half(b, hf):
                dve.wait_ge(oT_hi, 2 * b + (hf + 1))
                nc.vector.tensor_tensor(oT[:, hf, LO, :], flat[:, bass.ds(b * D + hf * BANK, BANK)],
                                        oT[:, hf, HI, :].bitcast(F32), ALU.subtract).then_inc(oT_ready, 1)

            def add_attention(b, odd):
                dve.wait_ge(wo_half, 2 * b + 2)
                dve.wait_ge(xr_in, 16 * b + 16)
                dve.wait_ge(oT_ready, 2 * b + 2)
                for c in range(NC):
                    nc.vector.tensor_tensor(flat[:, bass.ds(b * D + c * BANK, BANK)], ps[2 * odd + c][:],
                                            xr[:, c * BANK:(c + 1) * BANK], ALU.add).then_inc(h_added, 1)

            def h_norm(b, bb):
                dve.wait_ge(gain_in, 32 if bb is b else 48)
                dve.wait_ge(h_rstd, bb + 1)
                nc.vector.scalar_tensor_tensor(out=hn[:], in0=flat[:, bass.ds(b * D, D)], scalar=row_rstd[:],
                                               in1=gain[:], op0=ALU.mult, op1=ALU.mult).then_inc(hn_ready, 1)

            def uT_lo_part(b, bb, banks):
                for hf in range(2):
                    dve.wait_ge(uT_hi, 2 * bb + (hf + 1))
                    nc.vector.tensor_tensor(uT[:, LO, 4 * hf:4 * hf + 4, bass.ds(b * P, P)],
                                            banks[hf][:].rearrange("p (k n) -> p k n", k=4),
                                            uT[:, HI, 4 * hf:4 * hf + 4, bass.ds(b * P, P)].bitcast(F32),
                                            ALU.subtract).then_inc(uT_ready, 1)

            def block_b(b, odd, first=False, last=False):
                if not last:
                    oT_lo_half(b + 1, 0)
                if not first:
                    uT_lo_part(b - 1, b - 1, b_banks(not odd))
                if not last:
                    oT_lo_half(b + 1, 1)
                add_attention(b, odd)
                h_norm(b, b)

            oT_lo_half(0, 0)
            oT_lo_half(0, 1)
            block_b(0, False, first=True)
            for k in range(2):
                lo_unit(w1_unit(0, k), "w1", k)
            with dve.Fori(0, (NB - 2) // 2) as i:
                block_b(2 * i + 1, True)
                block_b(2 * i + 2, False)
            for k in range(2, 4):
                lo_unit(w1_unit(0, k), "w1", k)
            block_b(NB - 1, True, last=True)

            def square(g, i):
                dve.wait_ge(z_relu, 8 * g + (i + 1))
                nc.vector.tensor_tensor(act_buf[:, i % 2, :], ps[i % 4][:], act_buf[:, i % 2, :],
                                        ALU.mult).then_inc(z_squared, 1)

            def hid_lo_part(g, i):
                cols = slice((i // MT) * BANK, (i // MT + 1) * BANK)
                dve.wait_ge(hid_hi, 8 * g + (i + 1))
                nc.vector.tensor_tensor(hid[:, LO, i % MT, cols], act_buf[:, i % 2, :],
                                        hid[:, HI, i % MT, cols].bitcast(F32), ALU.subtract).then_inc(hid_ready, 1)

            def add_group(g, b, c):
                dve.wait_ge(w2_done, 16 * g + (2 * b + c + 1))
                wait(dve, h_summed, 16 * g + (2 * b + c - 15))
                cols = slice(c * BANK, (c + 1) * BANK)
                nc.vector.tensor_tensor(RES[:, b, cols], ps[4 + (2 * b + c) % 4][:], RES[:, b, cols],
                                        ALU.add).then_inc(h_summed, 1)

            def group(g, first=False, last=False):
                for i in range(2 * MT):
                    square(g, i)
                    hid_lo_part(g, i)
                    if first and i == 0:
                        uT_lo_part(NB - 1, NB - 1, b_banks(True))
                    if i % 2 == 0:
                        lo_unit(w2_unit(g, i // 2), "w2", i // 2)
                for a in range(NB):
                    if a % 2 == 0:
                        lo_unit(w1_unit(g, a // 2) + 8, "w1", a // 2)
                    add_group(g, a, 0)
                    add_group(g, a, 1)
                    if last:
                        if a >= 1:
                            uT_lo_part(a - 1, NB + a - 1, d_banks((a - 1) % 2))
                        h_norm(a, NB + a)

            group(0, first=True)
            with dve.Fori(1, NG - 1) as g:
                group(g)
            group(NG - 1, last=True)

            def add_gated(s):
                c, b = s // NB, s % NB
                cols = slice(c * BANK, (c + 1) * BANK)
                dve.wait_ge(sig_ready, s + 1)
                dve.wait_ge(proj_done, s + 1)
                nc.vector.tensor_tensor(sig[:, s % 2, :], ps[6 + s % 2][:], sig[:, s % 2, :],
                                        ALU.mult).then_inc(gated, 1)
                dve.wait_ge(gated, s + 1)
                nc.vector.tensor_tensor(RES[:, b, cols], RES[:, b, cols], sig[:, s % 2, :],
                                        ALU.add).then_inc(out_ready, 1)

            uT_lo_part(NB - 1, 2 * NB - 1, d_banks(True))
            for q in range(4):
                cols = slice((q % 2) * BANK, (q % 2 + 1) * BANK)
                dve.wait_ge(eT_hi, q + 1)
                nc.vector.tensor_tensor(eT[:, LO, q // 2, cols], ps[q][:], eT[:, HI, q // 2, cols].bitcast(F32),
                                        ALU.subtract).then_inc(eT_ready, 1)
            for k in range(PT):
                lo_unit(U_PROJ + k, "proj", k)
            add_gated(0)
            add_gated(1)
            for s in range(2, NB * NC):
                if s < 6:
                    lo_unit(U_GATE1 + s - 2, "gate1", s - 2)
                add_gated(s)

        @block.tensor
        def _(pe):
            def turn_x(b):
                pe.wait_ge(ident_ready, 1)
                pe.wait_ge(xn_ready, b + 1)
                wait(pe, T_ready["q0"], b)
                for hf in range(2):
                    bank = ps[6] if hf == 0 else ps[1]
                    for k in range(4):
                        kt = 4 * hf + k
                        mm = nc.tensor.transpose(bank[:, k * P:(k + 1) * P], xn[:, kt * P:(kt + 1) * P], ident[:])
                    mm.then_inc(xT_done, 1)

            def project(X, b, first_block=False):
                pe.wait_ge(xT_ready, 2 * b + 2)
                if X == "kv":
                    wait(pe, normed["q8"], b)
                if X == "q8":
                    pe.wait_ge(normed["kv"], b + 1)
                    pe.wait_ge(v_staged, b + 1)
                at = {"kv": 2 * BANK, "q0": 0, "q8": BANK}[X]
                for kt in range(KT):
                    if first_block and X == "kv" and kt % 2 == 0:
                        pe.wait_ge(w_split, kt // 2 + 1)
                    if first_block and X == "q0":
                        pe.wait_ge(w_split, 4 + kt + 1)
                    for i, (s, m) in enumerate(PASSES):
                        mm = nc.tensor.matmul(proj_bank[X][:], xT[:, s, kt, :], wq[:, m, kt, at:at + BANK],
                                              start=(kt == 0 and i == 0), stop=(kt == KT - 1 and i == 2))
                mm.then_inc(projected[X], 1)

            def turn(X, b):
                pe.wait_ge(normed[X], b + 1)
                if X == "kv":
                    if isinstance(b, int) and b == 0:
                        pe.wait_ge(xT_ready, 1)
                    wait(pe, T_ready["q8"], b)
                if X == "q0":
                    pe.wait_ge(T_ready["kv"], b + 1)
                if X == "q8":
                    pe.wait_ge(T_ready["q0"], b + 1)
                    if not (isinstance(b, int) and b == NB - 1):
                        pe.wait_ge(xT_ready, 2 * b + 3)
                at = {"kv": H * HD, "q0": 0, "q8": BANK}[X]
                for a in range(2 if X == "kv" else 4):
                    mm = nc.tensor.transpose(tr_bank[:, a * P:(a + 1) * P], qkn[:, at + a * P:at + (a + 1) * P],
                                             ident[:])
                mm.then_inc(turned[X], 1)

            def scores(n, j):
                t = 4 * n + j
                pe.wait_ge(T_ready["q0" if j < 2 else "q8"], n + 1)
                pe.wait_ge(T_ready["kv"], n + 1)
                wait(pe, biased, 4 * t)
                rows = q_rows(j)
                for r in range(G):
                    dst = score_bank[r // 2][:, (r % 2) * 2 * P:(r % 2 + 1) * 2 * P]
                    for i, (s, m) in enumerate(PASSES):
                        mm = nc.tensor.matmul(dst, qT[rows, s, (j // 2) * G + r, :],
                                              kT[rows, 2 * m + j // 2, :, :].rearrange("p a n -> p (a n)"),
                                              start=(i == 0), stop=(i == 2))
                    if r % 2 == 1:
                        mm.then_inc(scores_ready, 1)

            def turn_probs(n, j):
                t = 4 * n + j
                pe.wait_ge(probs_ready, t + 1)
                wait(pe, pT_ready, 2 * t)
                for kt in range(2):
                    for r in range(G):
                        mm = nc.tensor.transpose(pT_bank[kt][:, pos(r) * P:(pos(r) + 1) * P],
                                                 probs[:, j % 2, r, kt * P:(kt + 1) * P], ident[:])
                    mm.then_inc(probs_turned, 1)

            def weigh_values(n, j):
                t = 4 * n + j
                pe.wait_ge(pT_ready, 2 * t + 2)
                pe.wait_ge(v_ready, n + 1)
                wait(pe, attended, t)
                done = 0
                for kt in range(2):
                    for s, m in PASSES:
                        for odd in range(2):
                            at = 2 * HD * j + (0 if odd else HD)
                            mm = nc.tensor.matmul(pv_bank[:, 0:2 * P], vz[:, kt, s, at:at + 2 * HD],
                                                  pT[:, m, kt, odd * 2 * P:(odd + 1) * 2 * P],
                                                  start=(done == 0), stop=(done == 11))
                            done += 1
                mm.then_inc(pv_done, 1)

            def before(n, j, lag):
                return (n, j - lag) if j >= lag else (n - 1, j - lag + GROUPS)

            def body(n, first=False, last=False):
                for j in range(GROUPS):
                    scores(n, j)
                    if not last:
                        if j == 1:
                            project("kv", n + 1)
                        if j == 2:
                            project("q0", n + 1)
                        if j == 3:
                            turn("kv", n + 1)
                            project("q8", n + 1)
                    if not (first and j < 2):
                        weigh_values(*before(n, j, 2))
                    if not (first and j < 1):
                        turn_probs(*before(n, j, 1))
                    if j == 0:
                        if not last:
                            turn_x(n + 1)
                        turn("q8", n)
                    if j == 3 and not last:
                        turn("q0", n + 1)

            turn_x(0)
            project("kv", 0, first_block=True)
            project("q0", 0, first_block=True)
            turn("kv", 0)
            project("q8", 0)
            turn("q0", 0)
            body(0, first=True)
            with pe.Fori(1, NB - 1) as n:
                body(n)
            body(NB - 1, last=True)
            weigh_values(NB - 1, GROUPS - 2)
            turn_probs(NB - 1, GROUPS - 1)
            weigh_values(NB - 1, GROUPS - 1)

            def project_out(b, odd):
                wait(pe, h_added, 2 * b - 2)
                for hf in range(2):
                    if isinstance(b, int) and b == 0:
                        pe.wait_ge(w_split, U_WO + 4 * hf + 4)
                    pe.wait_ge(oT_ready, 2 * b + (hf + 1))
                    for k in range(4):
                        for c in range(NC):
                            for i, (s, m) in enumerate(PASSES):
                                mm = nc.tensor.matmul(ps[2 * odd + c][:], oT[:, hf, s, k * P:(k + 1) * P],
                                                      wo_s[:, m, 4 * hf + k, c * BANK:(c + 1) * BANK],
                                                      start=(hf == 0 and k == 0 and i == 0),
                                                      stop=(hf == 1 and k == 3 and i == 2))
                    mm.then_inc(wo_half, 1)

            def turn_h(b, bb, banks):
                pe.wait_ge(hn_ready, bb + 1)
                wait(pe, uT_ready, 2 * bb - 2)
                for hf in range(2):
                    for k in range(4):
                        kt = 4 * hf + k
                        mm = nc.tensor.transpose(banks[hf][:, k * P:(k + 1) * P], hn[:, kt * P:(kt + 1) * P], ident[:])
                    mm.then_inc(uT_done, 1)

            project_out(0, False)
            for b in (1, 2):
                project_out(b, b % 2)
                turn_h(b - 1, b - 1, b_banks(not b % 2))
            with pe.Fori(0, (NB - 4) // 2) as i:
                project_out(2 * i + 3, True)
                turn_h(2 * i + 2, 2 * i + 2, b_banks(False))
                project_out(2 * i + 4, False)
                turn_h(2 * i + 3, 2 * i + 3, b_banks(True))
            project_out(NB - 1, True)
            turn_h(NB - 2, NB - 2, b_banks(False))

            def group(g, first=False, last=False):
                for i in range(2 * MT):
                    th, m = i // MT, i % MT
                    if i == 0:
                        pe.wait_ge(w_split, w1_unit(g, 4))
                    if first and i == 0:
                        pe.wait_ge(h_added, 2 * NB)
                        pe.wait_ge(uT_ready, NB)
                    if first and i == MT:
                        pe.wait_ge(uT_ready, 2 * NB)
                    wait(pe, z_squared, 8 * g + (i - 3))
                    for kt in range(KT):
                        for q, (s, r) in enumerate(PASSES):
                            mm = nc.tensor.matmul(ps[i % 4][:], w1_s[:, s, kt, m * P:(m + 1) * P],
                                                  uT[:, r, kt, th * BANK:(th + 1) * BANK],
                                                  start=(kt == 0 and q == 0), stop=(kt == KT - 1 and q == 2))
                    mm.then_inc(z_ready, 1)
                    if first and i == 0:
                        turn_h(NB - 1, NB - 1, b_banks(True))
                for b in range(NB):
                    if b == 0:
                        pe.wait_ge(w_split, w2_unit(g, 4))
                        pe.wait_ge(hid_ready, 8 * g + MT)
                    if b == NB // 2:
                        pe.wait_ge(hid_ready, 8 * g + 2 * MT)
                    for c in range(NC):
                        a = 2 * b + c
                        wait(pe, h_summed, 16 * g + (a - 3))
                        for k in range(MT):
                            for q, (s, r) in enumerate(PASSES):
                                mm = nc.tensor.matmul(ps[4 + a % 4][:], hid[:, s, k, b * P:(b + 1) * P],
                                                      w2_s[:, r, k, c * BANK:(c + 1) * BANK],
                                                      start=(k == 0 and q == 0), stop=(k == MT - 1 and q == 2))
                        mm.then_inc(w2_done, 1)
                    if last and b >= 1:
                        turn_h(b - 1, NB + b - 1, d_banks((b - 1) % 2))

            group(0, first=True)
            with pe.Fori(1, NG - 1) as g:
                group(g)
            group(NG - 1, last=True)

            def gate(s):
                c, b = s // NB, s % NB
                if s == 0:
                    pe.wait_ge(h_summed, 16 * NG)
                    pe.wait_ge(w_split, U_GATE0 + 4)
                if s == NB:
                    pe.wait_ge(w_split, U_GATE1 + 4)
                if c == 0:
                    pe.wait_ge(uT_ready, 2 * NB + 2 * b + 2)
                wait(pe, sig_ready, s - 1)
                w = w1_s if c == 0 else g1_s
                for kt in range(KT):
                    for q, (u, m) in enumerate(PASSES):
                        mm = nc.tensor.matmul(ps[4 + s % 2][:], uT[:, u, kt, b * P:(b + 1) * P], w[:, m, kt, :],
                                              start=(kt == 0 and q == 0), stop=(kt == KT - 1 and q == 2))
                mm.then_inc(gate_done, 1)

            def embed(s):
                c, b = s // NB, s % NB
                if s == 0:
                    pe.wait_ge(eT_ready, 4)
                    pe.wait_ge(w_split, U_PROJ + PT)
                wait(pe, gated, s - 1)
                for k in range(PT):
                    for q, (u, m) in enumerate(PASSES):
                        mm = nc.tensor.matmul(ps[6 + s % 2][:], eT[:, u, k, b * P:(b + 1) * P],
                                              wp_s[:, m, k, c * BANK:(c + 1) * BANK],
                                              start=(k == 0 and q == 0), stop=(k == PT - 1 and q == 2))
                mm.then_inc(proj_done, 1)

            gate(0)
            turn_h(NB - 1, 2 * NB - 1, d_banks(True))
            gate(1)
            pe.wait_ge(emb_in, 16)
            pe.wait_ge(uT_ready, 4 * NB)
            for q in range(4):
                for i in range(4):
                    b = (q % 2) * 4 + i
                    mm = nc.tensor.transpose(ps[q][:, i * P:(i + 1) * P], emb[:, b, (q // 2) * P:(q // 2 + 1) * P],
                                             ident[:])
                mm.then_inc(emb_turned, 1)
            gate(2)
            embed(0)
            embed(1)
            embed(2)
            for s in range(3, NB * NC):
                gate(s)
                embed(s)


_INS = ["x", "p", "mix_norm_g", "mlp_norm_g", "ple_norm_g", "a_wqkv", "a_q_norm_g", "a_k_norm_g", "a_sinks",
        "a_wo", "m_w1", "m_w2", "ple_w_proj", "ple_w_gate"]


def kernel(**inputs):
    import numpy as np
    import concourse.bacc as bacc
    from concourse.bass_utils import run_bass_kernel_spmd

    shape = inputs["x"].shape
    nc = bacc.Bacc("TRN2", target_bir_lowering=False, num_devices=1, dynamic_dma_scratch_size=1024)
    arrays, args = {}, []
    for name in _INS:
        a = np.ascontiguousarray(inputs[name])
        a = a.reshape(a.shape[2:] if name == "p" else a.shape[1:])
        arrays[f"in_{name}"] = a
        args.append(nc.dram_tensor(f"in_{name}", a.shape, mybir.dt.from_np(a.dtype), kind="ExternalInput").ap())
    args.append(nc.dram_tensor("out", shape[1:], F32, kind="ExternalOutput").ap())
    trunk_layer(nc, *args)
    r = run_bass_kernel_spmd(nc, [arrays], core_ids=[0])
    return r.results[0]["out"].reshape(shape)
```

```python
from contextlib import ExitStack

import concourse.bass as bass
from concourse import mybir

F32 = mybir.dt.float32
F32R = mybir.dt.float32r
ALU = mybir.AluOpType
ACT = mybir.ActivationFunctionType
AX = mybir.AxisListType

P = 128
BANK = 512
EPS = 1e-6
WO_DVE, WO_POOL = (0, 2, 4, 6), (1, 3, 5, 7)
WARM_UP = 34
HI, LO = 0, 1
PASSES = ((HI, HI), (HI, LO), (LO, HI))
MASKED = -1e30
Q8_HEAD, Q8_TAIL = range(0, 6), range(6, 8)
PARTS = ("k", "q0", "q8")


def trunk_layer(nc, x, p, mix_g, mlp_g, ple_g, wqkv, gq, gk, sinks, wo, w1, w2, w_proj, w_gate, out):
    T, D = x.shape
    HD = gq.shape[0]
    H = sinks.shape[0]
    QKV = wqkv.shape[1]
    KV = (QKV // HD - H) // 2
    G = H // KV
    NB = T // P
    KT = D // P
    NG = w1.shape[1] // BANK
    MT = BANK // P
    PT = p.shape[1] // P
    NC = D // BANK
    GROUPS = KV
    assert (KT, NB, G, KV, HD, NG, PT, NC) == (8, 8, 4, 4, 64, 8, 2, 2)

    U_W1 = 12
    U_MLP = U_W1 + 4
    U_GATE0 = U_W1 + 8 * NG
    U_PROJ = U_GATE0 + 4
    U_GATE1 = U_PROJ + PT
    U_END = U_GATE1 + 4

    def w2_unit(g, k):
        return 8 * g + (U_MLP + k)

    def w1_unit(g, k):
        return 8 * g + (U_W1 + k)

    def rows_of(w, k, col, cols):
        return w[2 * k * P:(2 * k + 2) * P, bass.ds(col, cols)].rearrange("(k p) n -> p k n", p=P)

    with ExitStack() as ctx:
        def sem(name):
            return ctx.enter_context(nc.semaphore(name))

        def sb(name, shape, dt, where=ctx):
            return where.enter_context(nc.sbuf_tensor(name, shape, dt))

        WA = sb("WA", [P, 2 * 8192], F32R)
        first_wb = ExitStack()
        WB = sb("WB", [P, 8192], F32R, first_wb)
        first_wb.close()
        wo_raw = sb("wo_raw", [P, KT, D], F32)
        RES = sb("RES", [P, NB, D], F32)
        ring = sb("ring", [P, 2, D], F32)
        gain = sb("gain", [P, D], F32)
        ident = sb("ident", [P, P], F32)
        gq_col = sb("gq_col", [P, 1], F32)
        gq_s = sb("gq_s", [P, 1], F32)
        gk_col = sb("gk_col", [P, 1], F32)
        sink = sb("sink", [P, H], F32)
        nsink = sb("nsink", [P, H], F32)
        half = sb("half", [P, 8], F32)
        warm = sb("warm", [P, 1], F32)
        row_ssq = sb("row_ssq", [P, 1], F32)
        row_var = sb("row_var", [P, 1], F32)
        row_rstd = sb("row_rstd", [P, 1], F32)
        NH = {"k": KV, "q0": H // 2, "q8": H // 2}
        ssq = {X: sb(f"{X}_ssq", [P, NH[X]], F32) for X in PARTS}
        var = {X: sb(f"{X}_var", [P, NH[X]], F32) for X in PARTS}
        rstd = {X: sb(f"{X}_rstd", [P, NH[X]], F32) for X in PARTS}
        nmax = sb("nmax", [P, 2, G], F32)
        rmax = sb("rmax", [P, 2, G], F32)
        denom = sb("denom", [P, 2, G], F32)
        rden = sb("rden", [P, 2, G], F32)

        in_a = ExitStack()
        xT = sb("xT", [P, 2, KT, P], F32R, in_a)
        kn = sb("kn", [P, 2 * KV * HD], F32, in_a)
        qn = sb("qn", [P, H * HD], F32, in_a)
        qT = sb("qT", [P, H, P], F32R, in_a)
        kT = sb("kT", [P, 2, KV, 2, P], F32R, in_a)
        vnext = sb("vnext", [P, KV * HD], F32, in_a)
        vz = sb("vz", [P, 2, 2, (2 * KV + 1) * HD], F32R, in_a)
        probs = sb("probs", [P, 2, G, 2 * P + 2], F32, in_a)
        pT = sb("pT", [P, 2, 2, BANK], F32R, in_a)
        bias = sb("bias", [P, H, 2 * P], F32, in_a)
        dist = sb("dist", [P, 2 * P], F32, in_a)
        xn = sb("xn", [P, D], F32, in_a)
        xb = sb("xb", [P, D], F32, in_a)
        in_a.close()

        in_b = ExitStack()
        uT = sb("uT", [P, 2, KT, T], F32R, in_b)
        hn = sb("hn", [P, D], F32, in_b)
        only_b = ExitStack()
        xr = sb("xr", [P, D], F32, only_b)
        sb("gap", [P, 4 * G], F32, only_b)
        oT = sb("oT", [P, 2, 2, BANK], F32R, only_b)
        only_b.close()
        emb = sb("emb", [P, NB, PT * P], F32, in_b)
        act_buf = sb("act_buf", [P, 2, BANK], F32, in_b)
        in_b.close()
        sig = act_buf

        heads = {"k": kn, "q0": qn, "q8": qn}

        wq_q = WA[:].rearrange("p (s k n) -> p s k n", s=2, k=KT)
        wq_kv = WB[:].rearrange("p (s k n) -> p s k n", s=2, k=KT)
        wo_s = WA[:].rearrange("p (s k n) -> p s k n", s=2, k=KT)
        w1_s = WB[:].rearrange("p (s k n) -> p s k n", s=2, k=KT)
        w2_s = WA[:, 0:8192].rearrange("p (s k n) -> p s k n", s=2, k=MT)
        hid = WA[:, 8192:16384].rearrange("p (s k n) -> p s k n", s=2, k=MT)
        g1_s = WA[:, 0:8192].rearrange("p (s k n) -> p s k n", s=2, k=KT)
        wp_s = WA[:, 8192:12288].rearrange("p (s k n) -> p s k n", s=2, k=PT)
        eT = WA[:, 12288:16384].rearrange("p (s k n) -> p s k n", s=2, k=PT)

        ps = [ctx.enter_context(nc.psum_tensor(f"bank{i}", [P, BANK], F32)) for i in range(8)]
        pv_bank = ps[7]
        proj_bank = {"k": ps[0], "q0": ps[1], "q8": ps[0]}
        score_bank = (ps[2], ps[3])
        pT_bank = (ps[4], ps[5])
        tr_bank = (ps[6], ps[1])

        consts_in = sem("consts_in")
        gain_in = sem("gain_in")
        x_in = sem("x_in")
        raw_in = [sem(f"raw_in{i}") for i in range(8)]
        ring_in = [sem(f"ring_in{i}") for i in range(2)]
        emb_in = sem("emb_in")
        out_done = sem("out_done")
        ident_ready = sem("ident_ready")
        ident_zero = sem("ident_zero")
        half_ready = sem("half_ready")
        zeros_ready = sem("zeros_ready")
        dist_step = sem("dist_step")
        bias_first = sem("bias_first")
        bias_full = sem("bias_full")
        scales_ready = sem("scales_ready")
        w_hi = sem("w_hi")
        w_split = sem("w_split")
        wo_in = [sem(f"wo_in{k}") for k in range(KT)]
        wo_hi = sem("wo_hi")
        wo_lo = sem("wo_lo")
        wo_lo_pool = sem("wo_lo_pool")
        x_squared = sem("x_squared")
        x_var = sem("x_var")
        x_rstd = sem("x_rstd")
        xn_ready = sem("xn_ready")
        xT_done = sem("xT_done")
        xT_hi = sem("xT_hi")
        xT_ready = sem("xT_ready")
        projected = {X: sem(f"{X}_projected") for X in PARTS}
        squared = {X: sem(f"{X}_squared") for X in PARTS}
        summed = {X: sem(f"{X}_summed") for X in PARTS}
        var_ready = {X: sem(f"{X}_var_ready") for X in PARTS}
        rstd_ready = {X: sem(f"{X}_rstd_ready") for X in PARTS}
        normed = {X: sem(f"{X}_normed") for X in PARTS}
        turned = {X: sem(f"{X}_turned") for X in PARTS}
        T_hi = {X: sem(f"{X}_T_hi") for X in PARTS}
        T_ready = {X: sem(f"{X}_T_ready") for X in PARTS}
        k_shifted = sem("k_shifted")
        v_staged = sem("v_staged")
        v_shifted = sem("v_shifted")
        v_hi = sem("v_hi")
        v_ready = sem("v_ready")
        scores_ready = sem("scores_ready")
        biased = sem("biased")
        nmax_ready = sem("nmax_ready")
        sink_placed = sem("sink_placed")
        exps_done = sem("exps_done")
        rden_ready = sem("rden_ready")
        probs_ready = sem("probs_ready")
        probs_turned = sem("probs_turned")
        pT_hi = sem("pT_hi")
        pT_ready = sem("pT_ready")
        pv_done = sem("pv_done")
        attended = sem("attended")
        oT_hi = sem("oT_hi")
        oT_ready = sem("oT_ready")
        wo_half = sem("wo_half")
        xr_in = sem("xr_in")
        h_added = sem("h_added")
        h_squared = sem("h_squared")
        h_var = sem("h_var")
        h_rstd = sem("h_rstd")
        hn_ready = sem("hn_ready")
        uT_done = sem("uT_done")
        uT_hi = sem("uT_hi")
        uT_ready = sem("uT_ready")
        z_ready = sem("z_ready")
        z_relu = sem("z_relu")
        z_squared = sem("z_squared")
        hid_hi = sem("hid_hi")
        hid_ready = sem("hid_ready")
        w2_done = sem("w2_done")
        h_summed = sem("h_summed")
        emb_turned = sem("emb_turned")
        eT_hi = sem("eT_hi")
        eT_ready = sem("eT_ready")
        gate_done = sem("gate_done")
        proj_done = sem("proj_done")
        sig_ready = sem("sig_ready")
        gated = sem("gated")
        out_ready = sem("out_ready")

        passed = sem("passed")

        block = ctx.enter_context(nc.Block())

        def stand(eng, s, value):
            eng.wait_ge(s, value)
            if not isinstance(value, int):
                eng.sem_inc(passed, 1)

        def wait(eng, s, value):
            if not isinstance(value, int) or value > 0:
                eng.wait_ge(s, value)

        def split_to(kind, k, s):
            return {"kv": lambda: wq_kv[:, s, 2 * k:2 * k + 2, :],
                    "q0": lambda: wq_q[:, s, 2 * k:2 * k + 2, 0:BANK],
                    "q8": lambda: wq_q[:, s, 2 * k:2 * k + 2, BANK:D],
                    "w1": lambda: w1_s[:, s, 2 * k:2 * k + 2, :],
                    "w2": lambda: w2_s[:, s, k, :],
                    "gate1": lambda: g1_s[:, s, 2 * k:2 * k + 2, :],
                    "proj": lambda: wp_s[:, s, k, :]}[kind]()

        def shaped(raw, like):
            return raw if len(like.shape) == 2 else raw.rearrange("p (k n) -> p k n", k=like.shape[1])

        def pos(r):
            return (r % 2) * 2 + r // 2

        def turn_bank(X, hf):
            return ps[1] if X == "q0" and hf == 1 else ps[6]

        def b_banks(odd):
            return (ps[6], ps[7]) if odd else (ps[4], ps[5])

        def d_banks(odd):
            return (ps[2], ps[3]) if odd else (ps[0], ps[1])

        @block.sync
        def _(sp):
            def load_x(b):
                sp.wait_ge(xn_ready, b)
                sp.dma_start(xb[:], x[bass.ds(b * P, P), :]).then_inc(x_in, 16)

            sp.dma_start(xb[:], x[0:P, :]).then_inc(x_in, 16)
            for u in range(U_W1):
                if u == 4:
                    for col, g in ((gq_col, gq), (gk_col, gk)):
                        for a in range(2):
                            sp.dma_start(col[a * HD:(a + 1) * HD, :],
                                         g.rearrange("(d a) -> d a", a=1)).then_inc(consts_in, 16)
                    sp.dma_start(sink[:], sinks.partition_broadcast(P)).then_inc(consts_in, 16)
                if u >= 8:
                    sp.wait_ge(w_split, u - 8 + 1)
                col = (2 * BANK, 0, BANK)[u // 4]
                sp.dma_start(RES[:, u % 8, :].rearrange("p (k n) -> p k n", k=2),
                             rows_of(wqkv, u % 4, col, BANK)).then_inc(raw_in[u % 8], 16)
            with sp.Fori(1, NB) as b:
                load_x(b)
            sp.wait_ge(xn_ready, NB)
            sp.dma_start(gain[:], mlp_g.partition_broadcast(P)).then_inc(gain_in, 16)
            sp.wait_ge(projected["k"], NB)
            for k in range(KT):
                sp.dma_start(wo_raw[:, k, :], wo[k * P:(k + 1) * P, :]).then_inc(wo_in[k], 16)

            def load_residual(b):
                sp.wait_ge(h_added, 2 * b)
                sp.dma_start(xr[:], x[bass.ds(b * P, P), :]).then_inc(xr_in, 16)

            for k in range(4):
                if k >= 2:
                    sp.wait_ge(w_split, U_W1 + k - 1)
                else:
                    sp.wait_ge(w_split, U_W1)
                sp.dma_start(ring[:, k % 2, :].rearrange("p (k n) -> p k n", k=2),
                             rows_of(w1, k, 0, BANK)).then_inc(ring_in[k % 2], 16)
                if k == 1:
                    sp.wait_ge(biased, H * NB)
                    sp.dma_start(xr[:], x[0:P, :]).then_inc(xr_in, 16)
                    load_residual(1)
            with sp.Fori(2, NB) as b:
                load_residual(b)
            sp.wait_ge(wo_half, 2 * NB)
            sp.wait_ge(h_added, 2 * NB)
            sp.dma_start(emb[:], p.rearrange("(b p) n -> p b n", p=P)).then_inc(emb_in, 16)
            sp.wait_ge(hn_ready, NB)
            sp.dma_start(gain[:], ple_g.partition_broadcast(P)).then_inc(gain_in, 16)

            def load_group(g, last):
                for k in range(MT):
                    sp.wait_ge(w_split, w2_unit(g, k) - 1)
                    sp.dma_start(ring[:, k % 2, :], w2[bass.ds(g * BANK + k * P, P), :]).then_inc(ring_in[k % 2], 16)
                for k in range(4):
                    sp.wait_ge(w_split, w1_unit(g, k) + 7)
                    src = rows_of(w_gate, k, 0, BANK) if last else rows_of(w1, k, g * BANK + BANK, BANK)
                    sp.dma_start(ring[:, k % 2, :].rearrange("p (k n) -> p k n", k=2), src).then_inc(ring_in[k % 2], 16)

            with sp.Fori(0, NG - 1) as g:
                load_group(g, False)
            load_group(NG - 1, True)
            for k in range(PT):
                sp.wait_ge(w_split, U_PROJ + k - 1)
                sp.dma_start(ring[:, k % 2, :], w_proj[k * P:(k + 1) * P, :]).then_inc(ring_in[k % 2], 16)
            for k in range(4):
                sp.wait_ge(w_split, U_GATE1 + k - 1)
                sp.dma_start(ring[:, k % 2, :].rearrange("p (k n) -> p k n", k=2),
                             rows_of(w_gate, k, BANK, BANK)).then_inc(ring_in[k % 2], 16)
            for s in range(NB * NC):
                c, b = s // NB, s % NB
                sp.wait_ge(out_ready, s + 1)
                sp.dma_start(out[b * P:(b + 1) * P, c * BANK:(c + 1) * BANK],
                             RES[:, b, c * BANK:(c + 1) * BANK]).then_inc(out_done, 16)
            sp.wait_ge(out_done, 16 * NB * NC)

        @block.gpsimd
        def _(pool):
            pool.memset(half[:], -0.5).then_inc(half_ready, 1)
            pool.memset(ident[:], 0.0).then_inc(ident_zero, 1)
            pool.wait_ge(ident_zero, 1)
            pool.affine_select(out=ident[:], in_=ident[:], compare_op=ALU.not_equal, fill=1.0,
                               base=0, pattern=[[-1, P]], channel_multiplier=1).then_inc(ident_ready, 1)
            pool.wait_ge(half_ready, 1)

            def row_norm(squares, var_sem, rstd_sem, b):
                stand(pool, squares, b + 1)
                pool.tensor_scalar(row_var[:], row_ssq[:], 1.0 / D, EPS, ALU.mult, ALU.add).then_inc(var_sem, 1)
                pool.wait_ge(var_sem, b + 1)
                pool.tensor_tensor(row_rstd[:], row_var[:], half[:, 0:1], ALU.pow).then_inc(rstd_sem, 1)

            def head_norm(X, b):
                stand(pool, summed[X], b + 1)
                pool.tensor_scalar(var[X][:], ssq[X][:], 1.0 / HD, EPS, ALU.mult, ALU.add).then_inc(var_ready[X], 1)
                pool.wait_ge(var_ready[X], b + 1)
                pool.tensor_tensor(rstd[X][:], var[X][:], half[:, 0:NH[X]], ALU.pow).then_inc(rstd_ready[X], 1)

            row_norm(x_squared, x_var, x_rstd, 0)
            pool.memset(vz[:].bitcast(F32), 0.0).then_inc(zeros_ready, 1)
            pool.memset(kT[:].bitcast(F32), 0.0).then_inc(zeros_ready, 1)
            pool.iota(dist[:], pattern=[[-1, 2 * P]], base=P, channel_multiplier=1,
                      allow_small_or_imprecise_dtypes=True).then_inc(dist_step, 1)
            pool.wait_ge(dist_step, 1)
            pool.affine_select(out=dist[:], in_=dist[:], compare_op=ALU.is_ge, fill=-1e3 * MASKED,
                               base=P, pattern=[[-1, 2 * P]], channel_multiplier=1).then_inc(dist_step, 1)
            pool.wait_ge(dist_step, 2)
            pool.affine_select(out=dist[:], in_=dist[:], compare_op=ALU.is_ge, fill=-1e3 * MASKED,
                               base=-1, pattern=[[1, 2 * P]], channel_multiplier=-1).then_inc(dist_step, 1)
            pool.wait_ge(dist_step, 3)

            def bias_of(h, cols, ready):
                slope = 2.0 ** (-8.0 * (h + 1) / H)
                pool.tensor_scalar(bias[:, h, cols], dist[:, cols], -slope, 1.0, ALU.mult, ALU.mult).then_inc(ready, 1)

            pool.memset(bias[:, :, 0:P], MASKED).then_inc(bias_first, 1)
            for h in range(H):
                if h == 10:
                    head_norm("k", 0)
                bias_of(h, slice(P, 2 * P), bias_first)
            head_norm("q0", 0)
            row_norm(x_squared, x_var, x_rstd, 1)

            def copy(to, what):
                return pool.tensor_scalar(to, what.bitcast(F32), 1.0, 1.0, ALU.mult, ALU.mult)

            def shift_k(b):
                stand(pool, scores_ready, 8 * b)
                copy(kT[:, :, :, 0, :].rearrange("p s v n -> p (s v) n"),
                     kT[:, :, :, 1, :].rearrange("p s v n -> p (s v) n")).then_inc(k_shifted, 1)

            def shift_v(b):
                stand(pool, pv_done, 4 * b)
                copy(vz[:, 0], vz[:, 1]).then_inc(v_shifted, 1)

            def wo_lo_unit(k):
                pool.wait_ge(wo_hi, k + 1)
                pool.tensor_tensor(wo_s[:, LO, k, :], wo_raw[:, k, :], wo_s[:, HI, k, :].bitcast(F32),
                                   ALU.subtract).then_inc(wo_lo_pool, 1)

            def place_sinks(n, j):
                t, i = 4 * n + j, j % 2
                if not isinstance(t, int) or t >= 2:
                    stand(pool, exps_done, t - 1)
                pool.tensor_scalar(probs[:, i, :, 2 * P], sink[:, G * j:G * j + G], 1.0, 1.0, ALU.mult,
                                   ALU.mult).then_inc(sink_placed, 1)

            def body(n, x_too=True, last=False):
                head_norm("q8", n)
                place_sinks(n, 1)
                place_sinks(n, 2)
                if last:
                    wo_lo_unit(WO_POOL[0])
                shift_v(n)
                if last:
                    wo_lo_unit(WO_POOL[1])
                if not last:
                    head_norm("q0", n + 1)
                if x_too and not last:
                    row_norm(x_squared, x_var, x_rstd, n + 2)
                place_sinks(n, 3)
                if not last:
                    head_norm("k", n + 1)
                    shift_k(n + 1)
                    place_sinks(n + 1, 0)

            pool.wait_ge(consts_in, 16 * 5)
            place_sinks(0, 0)
            place_sinks(0, 1)
            head_norm("q8", 0)
            for j in range(GROUPS):
                if j == 3:
                    shift_k(1)
                pool.wait_ge(biased, G * (j + 1))
                for r in range(G):
                    bias_of(G * j + r, slice(0, P), bias_full)
                if j == 0:
                    place_sinks(0, 2)
                if j == 1:
                    head_norm("q0", 1)
                    row_norm(x_squared, x_var, x_rstd, 2)
                    place_sinks(0, 3)
                if j == 2:
                    head_norm("k", 1)
            place_sinks(1, 0)
            with pool.Fori(1, NB - 2) as n:
                body(n)
            body(NB - 2, x_too=False)
            body(NB - 1, last=True)
            for k in WO_POOL[2:]:
                wo_lo_unit(k)
            with pool.Fori(0, 2 * NB) as b:
                row_norm(h_squared, h_var, h_rstd, b)

        @block.scalar
        def _(act):
            def hi_unit(u, kind, k, free=()):
                for s, v in free:
                    wait(act, s, v)
                if isinstance(u, int) and u < U_W1:
                    act.wait_ge(raw_in[u % 8], 16 * (u // 8 + 1))
                    raw = RES[:, u % 8, :]
                else:
                    act.wait_ge(ring_in[k % 2], (u - (U_W1 + k % 2)) * 8 + 16)
                    raw = ring[:, k % 2, :]
                dst = split_to(kind, k, HI)
                nc.scalar.activation(dst, shaped(raw, dst), ACT.Copy).then_inc(w_hi, 1)

            def wo_hi_unit(k):
                act.wait_ge(projected["q8"], NB)
                act.wait_ge(wo_in[k], 16)
                nc.scalar.activation(wo_s[:, HI, k, :], wo_raw[:, k, :], ACT.Copy).then_inc(wo_hi, 1)

            def x_squares(b):
                act.wait_ge(x_in, 16 * (b + 1))
                wait(act, xT_done, 2 * b)
                nc.scalar.activation(xn[:], xb[:], ACT.Square, accum_out=row_ssq[:]).then_inc(x_squared, 1)

            def xT_hi_half(b, hf):
                act.wait_ge(xT_done, 2 * b + (1 + hf))
                wait(act, projected["q8"], b)
                nc.scalar.activation(xT[:, HI, 4 * hf:4 * hf + 4, :], tr_bank[hf][:].rearrange("p (k n) -> p k n", k=4),
                                     ACT.Copy).then_inc(xT_hi, 1)

            def part_squares(X, b):
                act.wait_ge(projected[X], b + 1)
                if isinstance(b, int) and b == 0:
                    if X == "q0":
                        act.wait_ge(turned["k"], 1)
                    if X == "q8":
                        act.wait_ge(summed["q0"], 1)
                elif X == "q0":
                    act.wait_ge(summed["q8"], b)
                elif X == "k":
                    act.wait_ge(summed["q0"], b + 1)
                else:
                    act.wait_ge(turned["k"], b + 1)
                cols = NH[X] * HD
                nc.scalar.activation(kn[:, 0:cols], proj_bank[X][:, 0:cols], ACT.Square).then_inc(squared[X], 1)

            def stage_v(b):
                act.wait_ge(projected["k"], b + 1)
                wait(act, v_ready, b)
                nc.scalar.activation(vnext[:], ps[0][:, KV * HD:2 * KV * HD], ACT.Copy).then_inc(v_staged, 1)

            def values(slot, s):
                return vz[:, slot, s, HD:(2 * KV + 1) * HD].rearrange("p (v a d) -> p v a d", v=KV, a=2)[:, :, 0, :]

            def v_hi_part(b):
                act.wait_ge(v_staged, b + 1)
                if isinstance(b, int) and b == 0:
                    act.wait_ge(zeros_ready, 2)
                wait(act, v_shifted, b)
                nc.scalar.activation(values(1, HI), vnext[:].rearrange("p (v d) -> p v d", v=KV),
                                     ACT.Copy).then_inc(v_hi, 1)

            def k_hi_part(b):
                act.wait_ge(turned["k"], b + 1)
                if isinstance(b, int) and b == 0:
                    act.wait_ge(zeros_ready, 2)
                wait(act, k_shifted, b)
                nc.scalar.activation(kT[:, HI, :, 1, :], ps[6][:].rearrange("p (a n) -> p a n", a=KV),
                                     ACT.Copy, scale=gk_col[:]).then_inc(T_hi["k"], 1)

            def q_hi_part(X, b, hf):
                j = (0 if X == "q0" else 2) + hf
                act.wait_ge(turned[X], 2 * b + (1 + hf))
                wait(act, scores_ready, 8 * b + (2 * j - 6))
                nc.scalar.activation(qT[:, G * j:G * j + G, :], turn_bank(X, hf)[:].rearrange("p (a n) -> p a n", a=G),
                                     ACT.Copy, scale=gq_s[:]).then_inc(T_hi[X], 1)

            def exps(n, j):
                t, i = 4 * n + j, j % 2
                act.wait_ge(nmax_ready, t + 1)
                act.wait_ge(sink_placed, t + 1)
                for r in range(G):
                    row = probs[:, i, r, 0:2 * P + 1]
                    ex = nc.scalar.activation(row, row, ACT.Exp, bias=nmax[:, i, r:r + 1],
                                              accum_out=denom[:, i, r:r + 1])
                ex.then_inc(exps_done, 1)

            def pT_hi_part(t):
                for kt in range(2):
                    act.wait_ge(probs_turned, 2 * t + (1 + kt))
                    wait(act, pv_done, t)
                    nc.scalar.activation(pT[:, HI, kt, :], pT_bank[kt][:], ACT.Copy).then_inc(pT_hi, 1)

            def attention_out(n, j):
                t = 4 * n + j
                act.wait_ge(w_split, U_W1)
                act.wait_ge(pv_done, t + 1)
                dst = RES[:].rearrange("p b n -> p (b n)")[:, bass.ds(n * D + j * 2 * P, 2 * P)]
                nc.scalar.activation(dst, pv_bank[:, 0:2 * P], ACT.Copy).then_inc(attended, 1)

            def before(n, j, lag):
                return (n, j - lag) if j >= lag else (n - 1, j - lag + GROUPS)

            def body(n, first=False, last=False, x_too=True):
                for j in range(GROUPS):
                    t = 4 * n + j
                    if j == 0:
                        part_squares("q8", n)
                        if not last:
                            xT_hi_half(n + 1, 0)
                            xT_hi_half(n + 1, 1)
                    if j == 3 and not last:
                        q_hi_part("q0", n + 1, 0)
                        q_hi_part("q0", n + 1, 1)
                    if j == 1 or j == 2:
                        q_hi_part("q8", n, j - 1)
                    if last and j == 0:
                        wo_hi_unit(0)
                        wo_hi_unit(1)
                    if last and j == 3:
                        oT_hi_half(1, 0)
                    exps(n, j)
                    if j == 1 and not last:
                        part_squares("q0", n + 1)
                    if j == 2 and not last:
                        part_squares("k", n + 1)
                        stage_v(n + 1)
                    if j == 3 and not last:
                        k_hi_part(n + 1)
                    if not (first and j < 2):
                        attention_out(*before(n, j, 2))
                    if not (first and j < 1):
                        pT_hi_part(t - 1)
                    if j == 1:
                        v_hi_part(n)
                    if j == 1 and x_too:
                        x_squares(n + 2)
                    if last and j < 3:
                        wo_hi_unit(2 * j + 2)
                        wo_hi_unit(2 * j + 3)
                    if isinstance(n, int) and n == NB - 2 and j == 1:
                        oT_hi_half(0, 0)
                        oT_hi_half(0, 1)

            def oT_hi_half(b, hf):
                if isinstance(b, int) and b < 3:
                    act.wait_ge(xT_done, 2 * NB)
                    act.wait_ge(attended, GROUPS * (b + 1))
                else:
                    act.wait_ge(attended, NB * GROUPS)
                wait(act, wo_half, 2 * b + (hf - 1))
                src = RES[:].rearrange("p b n -> p (b n)")[:, bass.ds(b * D + hf * BANK, BANK)]
                nc.scalar.activation(oT[:, hf, HI, :], src, ACT.Copy).then_inc(oT_hi, 1)

            act.dma_start(gain[:], mix_g.partition_broadcast(P)).then_inc(gain_in, 16)
            act.wait_ge(half_ready, 1)
            nc.scalar.activation(warm[:], half[:, 0:1], ACT.Exp)
            x_squares(0)
            hi_unit(0, "kv", 0)
            xT_hi_half(0, 0)
            xT_hi_half(0, 1)
            hi_unit(1, "kv", 1)
            hi_unit(2, "kv", 2)
            hi_unit(3, "kv", 3)
            hi_unit(4, "q0", 0)
            hi_unit(5, "q0", 1)
            part_squares("k", 0)
            stage_v(0)
            hi_unit(6, "q0", 2)
            hi_unit(7, "q0", 3)
            hi_unit(8, "q8", 0)
            hi_unit(9, "q8", 1)
            act.wait_ge(scales_ready, 1)
            k_hi_part(0)
            hi_unit(10, "q8", 2)
            part_squares("q0", 0)
            hi_unit(11, "q8", 3)
            x_squares(1)
            q_hi_part("q0", 0, 0)
            q_hi_part("q0", 0, 1)
            body(0, first=True)
            with act.Fori(1, NB - 2) as n:
                body(n)
            body(NB - 2, x_too=False)
            body(NB - 1, last=True, x_too=False)
            oT_hi_half(1, 1)
            attention_out(NB - 1, GROUPS - 2)
            pT_hi_part(NB * GROUPS - 1)
            oT_hi_half(2, 0)
            attention_out(NB - 1, GROUPS - 1)
            oT_hi_half(2, 1)

            def h_squares(b, summed_sem, base, bb):
                act.wait_ge(attended, NB * GROUPS)
                wait(act, uT_done, 2 * bb)
                stand(act, summed_sem, base + 2 * b + 2)
                src = RES[:].rearrange("p b n -> p (b n)")[:, bass.ds(b * D, D)]
                nc.scalar.activation(hn[:], src, ACT.Square, accum_out=row_ssq[:]).then_inc(h_squared, 1)

            def uT_hi_part(b, bb, banks):
                for hf in range(2):
                    act.wait_ge(pv_done, NB * GROUPS)
                    act.wait_ge(uT_done, 2 * bb + (hf + 1))
                    nc.scalar.activation(uT[:, HI, 4 * hf:4 * hf + 4, bass.ds(b * P, P)],
                                         banks[hf][:].rearrange("p (k n) -> p k n", k=4),
                                         ACT.Copy).then_inc(uT_hi, 1)

            def step(b, odd, last=False):
                if not last:
                    oT_hi_half(b + 1, 0)
                    oT_hi_half(b + 1, 1)
                uT_hi_part(b - 2, b - 2, b_banks(odd))
                h_squares(b - 1, h_added, 0, b - 1)

            h_squares(0, h_added, 0, 0)
            for k in range(2):
                hi_unit(w1_unit(0, k), "w1", k, [(wo_lo, len(WO_DVE)), (wo_lo_pool, len(WO_POOL))])
            step(2, False)
            with act.Fori(0, (NB - 4) // 2) as i:
                step(2 * i + 3, True)
                step(2 * i + 4, False)
            for k in range(2, 4):
                hi_unit(w1_unit(0, k), "w1", k)
            step(NB - 1, True, last=True)

            def relu(g, i):
                act.wait_ge(z_ready, 8 * g + (i + 1))
                wait(act, hid_ready, 8 * g + (i - 1))
                nc.scalar.activation(act_buf[:, i % 2, :], ps[i % 4][:], ACT.Relu).then_inc(z_relu, 1)

            def hid_hi_part(g, i):
                act.wait_ge(z_squared, 8 * g + (i + 1))
                wait(act, w2_done, 16 * g)
                nc.scalar.activation(hid[:, HI, i % MT, (i // MT) * BANK:(i // MT + 1) * BANK],
                                     act_buf[:, i % 2, :], ACT.Copy).then_inc(hid_hi, 1)

            def group(g, first=False, last=False):
                for i in range(2 * MT):
                    if first and i == 0:
                        act.wait_ge(wo_half, 2 * NB)
                    relu(g, i)
                    hid_hi_part(g, i)
                    if first and i == 0:
                        uT_hi_part(NB - 2, NB - 2, b_banks(False))
                        h_squares(NB - 1, h_added, 0, NB - 1)
                    if first and i == 1:
                        uT_hi_part(NB - 1, NB - 1, b_banks(True))
                    if i % 2 == 0:
                        hi_unit(w2_unit(g, i // 2), "w2", i // 2, [(w2_done, 16 * g)])
                for a in range(NB):
                    if a % 2 == 0:
                        hi_unit(w1_unit(g, a // 2) + 8, "w1", a // 2, [(z_ready, 8 * g + 8)])
                    if last:
                        if a >= 1:
                            uT_hi_part_d(a - 1)
                        h_squares(a, h_summed, 16 * g, NB + a)

            def uT_hi_part_d(b):
                uT_hi_part(b, NB + b, d_banks(b % 2))

            group(0, first=True)
            with act.Fori(1, NG - 1) as g:
                group(g)
            group(NG - 1, last=True)

            def gate(s):
                act.wait_ge(gate_done, s + 1)
                wait(act, out_ready, s - 1)
                if s < 2:
                    act.wait_ge(hid_ready, 8 * NG)
                nc.scalar.activation(sig[:, s % 2, :], ps[4 + s % 2][:], ACT.Sigmoid).then_inc(sig_ready, 1)

            gate(0)
            uT_hi_part_d(NB - 1)
            gate(1)
            for q in range(4):
                act.wait_ge(emb_turned, q + 1)
                act.wait_ge(w2_done, 16 * NG)
                nc.scalar.activation(eT[:, HI, q // 2, (q % 2) * BANK:(q % 2 + 1) * BANK], ps[q][:],
                                     ACT.Copy).then_inc(eT_hi, 1)
            for k in range(PT):
                hi_unit(U_PROJ + k, "proj", k, [(w2_done, 16 * NG)])
            for s in range(2, NB * NC):
                gate(s)
                if s < 6:
                    hi_unit(U_GATE1 + s - 2, "gate1", s - 2, [(w2_done, 16 * NG)])

        @block.vector
        def _(dve):
            def lo_unit(u, kind, k):
                raw = RES[:, u % 8, :] if isinstance(u, int) and u < U_W1 else ring[:, k % 2, :]
                dst, top = split_to(kind, k, LO), split_to(kind, k, HI)
                dve.wait_ge(w_hi, u + 1)
                nc.vector.tensor_tensor(dst, shaped(raw, dst), top.bitcast(F32), ALU.subtract).then_inc(w_split, 1)

            def x_norm(b):
                dve.wait_ge(x_rstd, b + 1)
                nc.vector.scalar_tensor_tensor(out=xn[:], in0=xb[:], scalar=row_rstd[:], in1=gain[:],
                                               op0=ALU.mult, op1=ALU.mult).then_inc(xn_ready, 1)

            def xT_lo_half(b, hf):
                dve.wait_ge(xT_hi, 2 * b + (1 + hf))
                nc.vector.tensor_tensor(xT[:, LO, 4 * hf:4 * hf + 4, :], tr_bank[hf][:].rearrange("p (k n) -> p k n", k=4),
                                        xT[:, HI, 4 * hf:4 * hf + 4, :].bitcast(F32),
                                        ALU.subtract).then_inc(xT_ready, 1)

            def head_sums(X, b):
                dve.wait_ge(squared[X], b + 1)
                cols = NH[X] * HD
                nc.vector.tensor_reduce(ssq[X][:], kn[:, 0:cols].rearrange("p (h d) -> p h d", d=HD), AX.X,
                                        ALU.add).then_inc(summed[X], 1)

            def head_scale(X, b):
                dve.wait_ge(rstd_ready[X], b + 1)
                if X == "k":
                    dve.wait_ge(v_staged, b + 1)
                if X == "q8":
                    dve.wait_ge(turned["q0"], 2 * b + 2)
                if X == "q0":
                    wait(dve, turned["q8"], 2 * b)
                cols = NH[X] * HD
                nc.vector.tensor_tensor(
                    heads[X][:].rearrange("p (h a d) -> p h a d", a=2, d=HD),
                    proj_bank[X][:, 0:cols].rearrange("p (h d) -> p h d", d=HD).unsqueeze(2)
                    .to_broadcast([P, NH[X], 2, HD]),
                    rstd[X][:].unsqueeze(2).unsqueeze(3).to_broadcast([P, NH[X], 2, HD]), ALU.mult
                ).then_inc(normed[X], 1)

            def k_lo_part(b):
                dve.wait_ge(T_hi["k"], b + 1)
                nc.vector.scalar_tensor_tensor(
                    out=kT[:, LO, :, 1, :], in0=ps[6][:].rearrange("p (a n) -> p a n", a=KV),
                    scalar=gk_col[:], in1=kT[:, HI, :, 1, :].bitcast(F32), op0=ALU.mult,
                    op1=ALU.subtract).then_inc(T_ready["k"], 1)

            def q_lo_part(X, b, hf):
                j = (0 if X == "q0" else 2) + hf
                low = qT[HD:P, G * j:G * j + G, :]
                dve.wait_ge(T_hi[X], 2 * b + (1 + hf))
                nc.vector.scalar_tensor_tensor(
                    out=low, in0=turn_bank(X, hf)[HD:P, :].rearrange("p (a n) -> p a n", a=G), scalar=gq_s[HD:P, :],
                    in1=low.bitcast(F32), op0=ALU.mult, op1=ALU.subtract).then_inc(T_ready[X], 1)

            def v_lo_part(b):
                def values(s):
                    return vz[:, 1, s, HD:(2 * KV + 1) * HD].rearrange("p (v a d) -> p v a d", v=KV, a=2)[:, :, 0, :]
                dve.wait_ge(v_hi, b + 1)
                nc.vector.tensor_tensor(values(LO), vnext[:].rearrange("p (v d) -> p v d", v=KV),
                                        values(HI).bitcast(F32), ALU.subtract).then_inc(v_ready, 1)

            def add_bias(n, j, first):
                t, i = 4 * n + j, j % 2
                for r in range(G):
                    if r == 0:
                        if first:
                            dve.wait_ge(bias_first, 1 + H)
                        else:
                            dve.wait_ge(bias_full, G * (j + 1))
                        wait(dve, probs_turned, 2 * t - 2)
                    if r % 2 == 0:
                        stand(dve, scores_ready, 2 * t + (1 + r // 2))
                    nc.vector.tensor_tensor_reduce(
                        probs[:, i, r, 0:2 * P], score_bank[r // 2][:, (r % 2) * 2 * P:(r % 2 + 1) * 2 * P],
                        bias[:, G * j + r, :], 1.0, 0.0, ALU.add, ALU.max, rmax[:, i, r:r + 1]).then_inc(biased, 1)
                dve.wait_ge(biased, 4 * t + 4)
                nc.vector.scalar_tensor_tensor(out=nmax[:, i, :], in0=rmax[:, i, :], scalar=-1.0,
                                               in1=nsink[:, G * j:G * j + G], op0=ALU.mult,
                                               op1=ALU.min).then_inc(nmax_ready, 1)

            def invert(n, j):
                t, i = 4 * n + j, j % 2
                dve.wait_ge(exps_done, t + 1)
                nc.vector.reciprocal(rden[:, i, :], denom[:, i, :]).then_inc(rden_ready, 1)

            def scale_probs(n, j):
                t, i = 4 * n + j, j % 2
                dve.wait_ge(rden_ready, t + 1)
                for r in range(G):
                    ts = nc.vector.tensor_scalar(probs[:, i, r, 0:2 * P], probs[:, i, r, 0:2 * P], rden[:, i, r:r + 1],
                                                 None, ALU.mult)
                ts.then_inc(probs_ready, 1)

            def pT_lo_part(t):
                for kt in range(2):
                    dve.wait_ge(pT_hi, 2 * t + (1 + kt))
                    nc.vector.tensor_tensor(pT[:, LO, kt, :], pT_bank[kt][:], pT[:, HI, kt, :].bitcast(F32),
                                            ALU.subtract).then_inc(pT_ready, 1)

            def body(n, first=False, last=False, x_too=True):
                for j in range(GROUPS):
                    t = 4 * n + j
                    if j == 0:
                        head_sums("q8", n)
                    add_bias(n, j, first)
                    if j == 0:
                        if not last:
                            xT_lo_half(n + 1, 0)
                            xT_lo_half(n + 1, 1)
                        head_scale("q8", n)
                    if j == 1:
                        q_lo_part("q8", n, 0)
                    if j == 2:
                        q_lo_part("q8", n, 1)
                        if x_too:
                            x_norm(n + 2)
                        if isinstance(n, int) and n == NB - 2:
                            oT_lo_half(0, 0)
                            oT_lo_half(0, 1)
                        if not last:
                            head_sums("k", n + 1)
                            head_scale("q0", n + 1)
                            head_scale("k", n + 1)
                    if j == 3 and not last:
                        q_lo_part("q0", n + 1, 0)
                        q_lo_part("q0", n + 1, 1)
                    if last and j == 3:
                        oT_lo_half(1, 0)
                    invert(n, j)
                    if last and j == 0:
                        wo_lo_unit(WO_DVE[0])
                    if j == 1 and not last:
                        head_sums("q0", n + 1)
                    scale_probs(n, j)
                    if j == 3 and not last:
                        k_lo_part(n + 1)
                    if not (first and j < 1):
                        pT_lo_part(t - 1)
                    if j == 1:
                        v_lo_part(n)
                    if last and j + 1 < len(WO_DVE):
                        wo_lo_unit(WO_DVE[j + 1])

            flat = RES[:].rearrange("p b n -> p (b n)")

            def wo_lo_unit(k):
                dve.wait_ge(wo_hi, k + 1)
                nc.vector.tensor_tensor(wo_s[:, LO, k, :], wo_raw[:, k, :], wo_s[:, HI, k, :].bitcast(F32),
                                        ALU.subtract).then_inc(wo_lo, 1)

            def oT_lo_half(b, hf):
                dve.wait_ge(oT_hi, 2 * b + (hf + 1))
                nc.vector.tensor_tensor(oT[:, hf, LO, :], flat[:, bass.ds(b * D + hf * BANK, BANK)],
                                        oT[:, hf, HI, :].bitcast(F32), ALU.subtract).then_inc(oT_ready, 1)

            dve.wait_ge(gain_in, 16)
            x_norm(0)
            lo_unit(0, "kv", 0)
            xT_lo_half(0, 0)
            xT_lo_half(0, 1)
            lo_unit(1, "kv", 1)
            lo_unit(2, "kv", 2)
            lo_unit(3, "kv", 3)
            lo_unit(4, "q0", 0)
            lo_unit(5, "q0", 1)
            dve.wait_ge(consts_in, 16 * 5)
            nc.vector.tensor_scalar(nsink[:], sink[:], -1.0, None, ALU.mult)
            nc.vector.tensor_scalar(gq_s[:], gq_col[:], HD ** -0.5, None, ALU.mult).then_inc(scales_ready, 1)
            head_sums("k", 0)
            lo_unit(6, "q0", 2)
            lo_unit(7, "q0", 3)
            head_scale("k", 0)
            lo_unit(8, "q8", 0)
            k_lo_part(0)
            lo_unit(9, "q8", 1)
            head_sums("q0", 0)
            lo_unit(10, "q8", 2)
            lo_unit(11, "q8", 3)
            head_scale("q0", 0)
            x_norm(1)
            q_lo_part("q0", 0, 0)
            q_lo_part("q0", 0, 1)
            body(0, first=True)
            with dve.Fori(1, NB - 2) as n:
                body(n)
            body(NB - 2, x_too=False)
            body(NB - 1, last=True, x_too=False)
            oT_lo_half(1, 1)
            pT_lo_part(NB * GROUPS - 1)

            def add_attention(b, odd):
                dve.wait_ge(wo_half, 2 * b + 2)
                dve.wait_ge(xr_in, 16 * b + 16)
                dve.wait_ge(oT_ready, 2 * b + 2)
                for c in range(NC):
                    nc.vector.tensor_tensor(flat[:, bass.ds(b * D + c * BANK, BANK)], ps[2 * odd + c][:],
                                            xr[:, c * BANK:(c + 1) * BANK], ALU.add).then_inc(h_added, 1)

            def h_norm(b, bb, gains):
                dve.wait_ge(gain_in, 16 * gains)
                dve.wait_ge(h_rstd, bb + 1)
                nc.vector.scalar_tensor_tensor(out=hn[:], in0=flat[:, bass.ds(b * D, D)], scalar=row_rstd[:],
                                               in1=gain[:], op0=ALU.mult, op1=ALU.mult).then_inc(hn_ready, 1)

            def uT_lo_part(b, bb, banks):
                for hf in range(2):
                    dve.wait_ge(uT_hi, 2 * bb + (hf + 1))
                    nc.vector.tensor_tensor(uT[:, LO, 4 * hf:4 * hf + 4, bass.ds(b * P, P)],
                                            banks[hf][:].rearrange("p (k n) -> p k n", k=4),
                                            uT[:, HI, 4 * hf:4 * hf + 4, bass.ds(b * P, P)].bitcast(F32),
                                            ALU.subtract).then_inc(uT_ready, 1)

            def step(b, odd, last=False):
                if not last:
                    oT_lo_half(b + 1, 0)
                    oT_lo_half(b + 1, 1)
                add_attention(b, odd)
                uT_lo_part(b - 2, b - 2, b_banks(odd))
                h_norm(b - 1, b - 1, 2)

            add_attention(0, False)
            oT_lo_half(2, 0)
            oT_lo_half(2, 1)
            h_norm(0, 0, 2)
            add_attention(1, True)
            for k in range(2):
                lo_unit(w1_unit(0, k), "w1", k)
            step(2, False)
            with dve.Fori(0, (NB - 4) // 2) as i:
                step(2 * i + 3, True)
                step(2 * i + 4, False)
            for k in range(2, 4):
                lo_unit(w1_unit(0, k), "w1", k)
            step(NB - 1, True, last=True)

            def square(g, i):
                dve.wait_ge(z_relu, 8 * g + (i + 1))
                nc.vector.tensor_tensor(act_buf[:, i % 2, :], ps[i % 4][:], act_buf[:, i % 2, :],
                                        ALU.mult).then_inc(z_squared, 1)

            def hid_lo_part(g, i):
                cols = slice((i // MT) * BANK, (i // MT + 1) * BANK)
                dve.wait_ge(hid_hi, 8 * g + (i + 1))
                nc.vector.tensor_tensor(hid[:, LO, i % MT, cols], act_buf[:, i % 2, :],
                                        hid[:, HI, i % MT, cols].bitcast(F32), ALU.subtract).then_inc(hid_ready, 1)

            def add_group(g, b, c):
                dve.wait_ge(w2_done, 16 * g + (2 * b + c + 1))
                wait(dve, h_summed, 16 * g + (2 * b + c - 15))
                cols = slice(c * BANK, (c + 1) * BANK)
                nc.vector.tensor_tensor(RES[:, b, cols], ps[4 + (2 * b + c) % 4][:], RES[:, b, cols],
                                        ALU.add).then_inc(h_summed, 1)

            def group(g, first=False, last=False):
                for i in range(2 * MT):
                    square(g, i)
                    hid_lo_part(g, i)
                    if first and i == 0:
                        uT_lo_part(NB - 2, NB - 2, b_banks(False))
                        h_norm(NB - 1, NB - 1, 2)
                    if first and i == 1:
                        uT_lo_part(NB - 1, NB - 1, b_banks(True))
                    if i % 2 == 0:
                        lo_unit(w2_unit(g, i // 2), "w2", i // 2)
                for a in range(NB):
                    if a % 2 == 0:
                        lo_unit(w1_unit(g, a // 2) + 8, "w1", a // 2)
                    add_group(g, a, 0)
                    add_group(g, a, 1)
                    if last:
                        if a >= 1:
                            uT_lo_part(a - 1, NB + a - 1, d_banks((a - 1) % 2))
                        h_norm(a, NB + a, 3)

            group(0, first=True)
            with dve.Fori(1, NG - 1) as g:
                group(g)
            group(NG - 1, last=True)

            def add_gated(s):
                c, b = s // NB, s % NB
                cols = slice(c * BANK, (c + 1) * BANK)
                dve.wait_ge(sig_ready, s + 1)
                dve.wait_ge(proj_done, s + 1)
                nc.vector.tensor_tensor(sig[:, s % 2, :], ps[6 + s % 2][:], sig[:, s % 2, :],
                                        ALU.mult).then_inc(gated, 1)
                dve.wait_ge(gated, s + 1)
                nc.vector.tensor_tensor(RES[:, b, cols], RES[:, b, cols], sig[:, s % 2, :],
                                        ALU.add).then_inc(out_ready, 1)

            uT_lo_part(NB - 1, 2 * NB - 1, d_banks(True))
            for q in range(4):
                cols = slice((q % 2) * BANK, (q % 2 + 1) * BANK)
                dve.wait_ge(eT_hi, q + 1)
                nc.vector.tensor_tensor(eT[:, LO, q // 2, cols], ps[q][:], eT[:, HI, q // 2, cols].bitcast(F32),
                                        ALU.subtract).then_inc(eT_ready, 1)
            for k in range(PT):
                lo_unit(U_PROJ + k, "proj", k)
            add_gated(0)
            add_gated(1)
            for s in range(2, NB * NC):
                if s < 6:
                    lo_unit(U_GATE1 + s - 2, "gate1", s - 2)
                add_gated(s)

        @block.tensor
        def _(pe):
            def turn_x(b):
                pe.wait_ge(ident_ready, 1)
                pe.wait_ge(xn_ready, b + 1)
                wait(pe, T_ready["k"], b)
                wait(pe, T_ready["q0"], 2 * b)
                for hf in range(2):
                    for k in range(4):
                        kt = 4 * hf + k
                        mm = nc.tensor.transpose(tr_bank[hf][:, k * P:(k + 1) * P], xn[:, kt * P:(kt + 1) * P], ident[:])
                    mm.then_inc(xT_done, 1)

            def project(X, b, first_block=False, kts=range(KT)):
                pe.wait_ge(xT_ready, 2 * b + 2)
                if X == "k":
                    wait(pe, normed["q8"], b)
                if X == "q8":
                    pe.wait_ge(normed["k"], b + 1)
                w, at = {"k": (wq_kv, 0), "q0": (wq_q, 0), "q8": (wq_q, BANK)}[X]
                for kt in kts:
                    if first_block and kt % 2 == 0:
                        pe.wait_ge(w_split, 4 * PARTS.index(X) + kt // 2 + 1)
                    for i, (s, m) in enumerate(PASSES):
                        mm = nc.tensor.matmul(proj_bank[X][:], xT[:, s, kt, :], w[:, m, kt, at:at + BANK],
                                              start=(kt == 0 and i == 0), stop=(kt == KT - 1 and i == 2))
                if kts[-1] == KT - 1:
                    mm.then_inc(projected[X], 1)

            def turn_k(b):
                pe.wait_ge(normed["k"], b + 1)
                if isinstance(b, int) and b == 0:
                    pe.wait_ge(xT_ready, 2)
                else:
                    pe.wait_ge(T_ready["q0"], 2 * b + 1)
                for v in range(KV):
                    mm = nc.tensor.transpose(ps[6][:, v * P:(v + 1) * P], kn[:, v * P:(v + 1) * P], ident[:])
                mm.then_inc(turned["k"], 1)

            def turn_q(X, b, hf, after_x=True):
                pe.wait_ge(normed[X], b + 1)
                if X == "q0" and hf == 0:
                    if isinstance(b, int) and b == 0:
                        pe.wait_ge(T_ready["k"], 1)
                    wait(pe, T_ready["q8"], 2 * b)
                if X == "q8" and hf == 0:
                    pe.wait_ge(T_ready["k"], b + 1)
                    if after_x:
                        pe.wait_ge(xT_ready, 2 * b + 3)
                if X == "q8" and hf == 1:
                    pe.wait_ge(T_ready["q8"], 2 * b + 1)
                for a in range(4):
                    mm = nc.tensor.transpose(turn_bank(X, hf)[:, a * P:(a + 1) * P],
                                             qn[:, (4 * hf + a) * P:(4 * hf + a + 1) * P], ident[:])
                mm.then_inc(turned[X], 1)

            def scores(n, j):
                t = 4 * n + j
                pe.wait_ge(T_ready["q0" if j < 2 else "q8"], 2 * n + (1 + j % 2))
                pe.wait_ge(T_ready["k"], n + 1)
                wait(pe, biased, 4 * t)
                for r in range(G):
                    dst = score_bank[r // 2][:, (r % 2) * 2 * P:(r % 2 + 1) * 2 * P]
                    for m in (HI, LO):
                        mm = nc.tensor.matmul(dst, qT[:, G * j + r, :], kT[:, m, j, :, :].rearrange("p a n -> p (a n)"),
                                              start=(m == HI), stop=(m == LO))
                    if r % 2 == 1:
                        mm.then_inc(scores_ready, 1)

            def turn_probs(n, j):
                t = 4 * n + j
                pe.wait_ge(probs_ready, t + 1)
                wait(pe, pT_ready, 2 * t)
                for kt in range(2):
                    for r in range(G):
                        mm = nc.tensor.transpose(pT_bank[kt][:, pos(r) * P:(pos(r) + 1) * P],
                                                 probs[:, j % 2, r, kt * P:(kt + 1) * P], ident[:])
                    mm.then_inc(probs_turned, 1)

            def weigh_values(n, j):
                t = 4 * n + j
                pe.wait_ge(pT_ready, 2 * t + 2)
                pe.wait_ge(v_ready, n + 1)
                wait(pe, attended, t)
                done = 0
                for kt in range(2):
                    for s, m in PASSES:
                        for odd in range(2):
                            at = 2 * HD * j + (0 if odd else HD)
                            mm = nc.tensor.matmul(pv_bank[:, 0:2 * P], vz[:, kt, s, at:at + 2 * HD],
                                                  pT[:, m, kt, odd * 2 * P:(odd + 1) * 2 * P],
                                                  start=(done == 0), stop=(done == 11))
                            done += 1
                mm.then_inc(pv_done, 1)

            def before(n, j, lag):
                return (n, j - lag) if j >= lag else (n - 1, j - lag + GROUPS)

            def body(n, first=False, last=False):
                for j in range(GROUPS):
                    if j == 0 and not last:
                        project("q8", n, first_block=first, kts=Q8_TAIL)
                    scores(n, j)
                    if j == 0 and not last:
                        turn_x(n + 1)
                    if j == 1:
                        if not last:
                            project("q0", n + 1, kts=range(0, 5))
                        turn_q("q8", n, 0, after_x=not last)
                        if not last:
                            project("q0", n + 1, kts=range(5, KT))
                    if j == 2:
                        if not last:
                            project("k", n + 1, kts=range(0, 4))
                        turn_q("q8", n, 1)
                        if not last:
                            project("k", n + 1, kts=range(4, KT))
                    if j == 3 and not last:
                        turn_q("q0", n + 1, 0)
                        turn_q("q0", n + 1, 1)
                        project("q8", n + 1, kts=range(KT) if isinstance(n, int) and n == NB - 2 else Q8_HEAD)
                        turn_k(n + 1)
                    if last and j >= 1:
                        project_out(0, False, ks=range(2 * j - 2, 2 * j))
                    if not (first and j < 2):
                        weigh_values(*before(n, j, 2))
                    if not (first and j < 1):
                        turn_probs(*before(n, j, 1))

            def project_out(b, odd, ks=range(KT)):
                if isinstance(b, int) and b == 0:
                    pe.wait_ge(normed["q8"], NB)
                    pe.wait_ge(T_ready["q0"], 2 * NB)
                if isinstance(b, int) and b == 1:
                    pe.wait_ge(biased, H * NB)
                wait(pe, h_added, 2 * b - 2)
                for k in ks:
                    hf = k // 4
                    if k == ks[0] or k == 4:
                        pe.wait_ge(oT_ready, 2 * b + (hf + 1))
                    if isinstance(b, int) and b == 0:
                        if k in WO_DVE:
                            pe.wait_ge(wo_lo, WO_DVE.index(k) + 1)
                        else:
                            pe.wait_ge(wo_lo_pool, WO_POOL.index(k) + 1)
                    for c in range(NC):
                        for i, (s, m) in enumerate(PASSES):
                            mm = nc.tensor.matmul(ps[2 * odd + c][:], oT[:, hf, s, k % 4 * P:(k % 4 + 1) * P],
                                                  wo_s[:, m, k, c * BANK:(c + 1) * BANK],
                                                  start=(k == 0 and i == 0), stop=(k == KT - 1 and i == 2))
                    if k % 4 == 3:
                        mm.then_inc(wo_half, 1)

            def warm_up(count):
                pe.wait_ge(ident_ready, 1)
                for _ in range(count):
                    nc.tensor.transpose(ps[2][:, 0:P], ident[:], ident[:])

            warm_up(WARM_UP)
            turn_x(0)
            warm_up(WARM_UP // 4)
            project("k", 0, first_block=True)
            project("q0", 0, first_block=True, kts=range(0, 6))
            turn_k(0)
            project("q0", 0, first_block=True, kts=range(6, KT))
            project("q8", 0, first_block=True, kts=Q8_HEAD)
            turn_q("q0", 0, 0)
            turn_q("q0", 0, 1)
            body(0, first=True)
            with pe.Fori(1, NB - 2) as n:
                body(n)
            body(NB - 2)
            body(NB - 1, last=True)
            project_out(0, False, ks=range(6, KT))
            project_out(1, True, ks=range(0, 2))
            weigh_values(NB - 1, GROUPS - 2)
            turn_probs(NB - 1, GROUPS - 1)
            project_out(1, True, ks=range(2, 4))
            weigh_values(NB - 1, GROUPS - 1)
            project_out(1, True, ks=range(4, KT))

            def turn_h(b, bb, banks):
                pe.wait_ge(hn_ready, bb + 1)
                if isinstance(bb, int) and bb < 2:
                    pe.wait_ge(pT_ready, 2 * NB * GROUPS)
                    pe.wait_ge(attended, NB * GROUPS)
                wait(pe, uT_ready, 2 * bb - 2)
                for hf in range(2):
                    for k in range(4):
                        kt = 4 * hf + k
                        mm = nc.tensor.transpose(banks[hf][:, k * P:(k + 1) * P], hn[:, kt * P:(kt + 1) * P], ident[:])
                    mm.then_inc(uT_done, 1)

            def step(b, odd):
                project_out(b, odd)
                turn_h(b - 2, b - 2, b_banks(odd))

            step(2, False)
            step(3, True)
            with pe.Fori(0, (NB - 4) // 2) as i:
                step(2 * i + 4, False)
                step(2 * i + 5, True)

            def group(g, first=False, last=False):
                for i in range(2 * MT):
                    th, m = i // MT, i % MT
                    if i == 0:
                        pe.wait_ge(w_split, w1_unit(g, 4))
                    if first and i == 0:
                        pe.wait_ge(h_added, 2 * NB - 2)
                        pe.wait_ge(uT_ready, NB)
                    if first and i == 2:
                        pe.wait_ge(h_added, 2 * NB)
                    if first and i == MT:
                        pe.wait_ge(uT_ready, 2 * NB)
                    wait(pe, z_squared, 8 * g + (i - 3))
                    for kt in range(KT):
                        for q, (s, r) in enumerate(PASSES):
                            mm = nc.tensor.matmul(ps[i % 4][:], w1_s[:, s, kt, m * P:(m + 1) * P],
                                                  uT[:, r, kt, th * BANK:(th + 1) * BANK],
                                                  start=(kt == 0 and q == 0), stop=(kt == KT - 1 and q == 2))
                    mm.then_inc(z_ready, 1)
                    if first and i == 0:
                        turn_h(NB - 2, NB - 2, b_banks(False))
                    if first and i == 1:
                        turn_h(NB - 1, NB - 1, b_banks(True))
                for b in range(NB):
                    if b == 0:
                        pe.wait_ge(w_split, w2_unit(g, 4))
                        pe.wait_ge(hid_ready, 8 * g + MT)
                    if b == NB // 2:
                        pe.wait_ge(hid_ready, 8 * g + 2 * MT)
                    for c in range(NC):
                        a = 2 * b + c
                        wait(pe, h_summed, 16 * g + (a - 3))
                        for k in range(MT):
                            for q, (s, r) in enumerate(PASSES):
                                mm = nc.tensor.matmul(ps[4 + a % 4][:], hid[:, s, k, b * P:(b + 1) * P],
                                                      w2_s[:, r, k, c * BANK:(c + 1) * BANK],
                                                      start=(k == 0 and q == 0), stop=(k == MT - 1 and q == 2))
                        mm.then_inc(w2_done, 1)
                    if last and b >= 1:
                        turn_h(b - 1, NB + b - 1, d_banks((b - 1) % 2))

            group(0, first=True)
            with pe.Fori(1, NG - 1) as g:
                group(g)
            group(NG - 1, last=True)

            def gate(s):
                c, b = s // NB, s % NB
                if s == 0:
                    pe.wait_ge(h_summed, 16 * NG)
                    pe.wait_ge(w_split, U_GATE0 + 4)
                if s == NB:
                    pe.wait_ge(w_split, U_GATE1 + 4)
                if c == 0:
                    pe.wait_ge(uT_ready, 2 * NB + 2 * b + 2)
                wait(pe, sig_ready, s - 1)
                w = w1_s if c == 0 else g1_s
                for kt in range(KT):
                    for q, (u, m) in enumerate(PASSES):
                        mm = nc.tensor.matmul(ps[4 + s % 2][:], uT[:, u, kt, b * P:(b + 1) * P], w[:, m, kt, :],
                                              start=(kt == 0 and q == 0), stop=(kt == KT - 1 and q == 2))
                mm.then_inc(gate_done, 1)

            def embed(s):
                c, b = s // NB, s % NB
                if s == 0:
                    pe.wait_ge(eT_ready, 4)
                    pe.wait_ge(w_split, U_PROJ + PT)
                wait(pe, gated, s - 1)
                for k in range(PT):
                    for q, (u, m) in enumerate(PASSES):
                        mm = nc.tensor.matmul(ps[6 + s % 2][:], eT[:, u, k, b * P:(b + 1) * P],
                                              wp_s[:, m, k, c * BANK:(c + 1) * BANK],
                                              start=(k == 0 and q == 0), stop=(k == PT - 1 and q == 2))
                mm.then_inc(proj_done, 1)

            gate(0)
            turn_h(NB - 1, 2 * NB - 1, d_banks(True))
            gate(1)
            pe.wait_ge(emb_in, 16)
            pe.wait_ge(uT_ready, 4 * NB)
            for q in range(4):
                for i in range(4):
                    b = (q % 2) * 4 + i
                    mm = nc.tensor.transpose(ps[q][:, i * P:(i + 1) * P], emb[:, b, (q // 2) * P:(q // 2 + 1) * P],
                                             ident[:])
                mm.then_inc(emb_turned, 1)
            gate(2)
            embed(0)
            embed(1)
            embed(2)
            for s in range(3, NB * NC):
                gate(s)
                embed(s)


_INS = ["x", "p", "mix_norm_g", "mlp_norm_g", "ple_norm_g", "a_wqkv", "a_q_norm_g", "a_k_norm_g", "a_sinks",
        "a_wo", "m_w1", "m_w2", "ple_w_proj", "ple_w_gate"]


def kernel(**inputs):
    import numpy as np
    import concourse.bacc as bacc
    from concourse.bass_utils import run_bass_kernel_spmd

    shape = inputs["x"].shape
    nc = bacc.Bacc("TRN2", target_bir_lowering=False, num_devices=1, dynamic_dma_scratch_size=1024)
    arrays, args = {}, []
    for name in _INS:
        a = np.ascontiguousarray(inputs[name])
        a = a.reshape(a.shape[2:] if name == "p" else a.shape[1:])
        arrays[f"in_{name}"] = a
        args.append(nc.dram_tensor(f"in_{name}", a.shape, mybir.dt.from_np(a.dtype), kind="ExternalInput").ap())
    args.append(nc.dram_tensor("out", shape[1:], F32, kind="ExternalOutput").ap())
    trunk_layer(nc, *args)
    r = run_bass_kernel_spmd(nc, [arrays], core_ids=[0])
    return r.results[0]["out"].reshape(shape)
```
